# Optimizing a Trainium2 kernel written in Bass

```python
import jax
import jax.numpy as jnp
from jax import lax
import numpy as np
import math
import jax, jax.numpy as jnp

D_MODEL = 1024
BATCH = 1
SEQ = 512
DEPTH = 2

GRID_W = 64
CTX_LEN = 256
N_MIXERS = 2
N_ATTN_LAYERS = (DEPTH + N_MIXERS - 1) // N_MIXERS
N_RET_LAYERS = DEPTH // N_MIXERS

HEAD_DIM = 64
N_HEADS = D_MODEL // HEAD_DIM
N_KV_HEADS = N_HEADS // 4
GQA_GROUP = N_HEADS // N_KV_HEADS
WINDOW = 128
ATTN_BLOCK = 128
ATTN_PROJ = (N_HEADS + 2 * N_KV_HEADS) * HEAD_DIM

RET_HEADS = D_MODEL // 256
RET_QK_DIM = D_MODEL // RET_HEADS
RET_V_DIM = 2 * D_MODEL // RET_HEADS
RET_VWIDTH = 2 * D_MODEL
RET_CHUNK = 128
RET_PROJ = 2 * D_MODEL + 2 * RET_VWIDTH

D_FF = -(-8 * D_MODEL // (3 * 256)) * 256

ROPE_BASE = 10000.0
EPS = 1e-6
NEG_INF = -1e30


def rms_norm(x, g):
    xf = x.astype(jnp.float32)
    y = xf * lax.rsqrt(jnp.mean(xf * xf, axis=-1, keepdims=True) + EPS)
    return (y * g.astype(jnp.float32)).astype(x.dtype)

def modulate(h, shift, scale):
    return h * (1 + scale) + shift

def grid_positions(n):
    rows = n // GRID_W
    row = jnp.broadcast_to(jnp.arange(rows, dtype=jnp.int32)[:, None], (rows, GRID_W)).reshape(n)
    col = jnp.broadcast_to(jnp.arange(GRID_W, dtype=jnp.int32)[None, :], (rows, GRID_W)).reshape(n)
    return row, col

def rope_tables(n, head_dim):
    row, col = grid_positions(n)
    axis_dim = head_dim // 2
    inv = ROPE_BASE ** (-jnp.arange(0, axis_dim, 2, dtype=jnp.float32) / axis_dim)
    ang_r = row.astype(jnp.float32)[:, None] * inv
    ang_c = col.astype(jnp.float32)[:, None] * inv
    return jnp.cos(ang_r), jnp.sin(ang_r), jnp.cos(ang_c), jnp.sin(ang_c)

def rotate_axis(x, cos, sin):
    x1, x2 = jnp.split(x, 2, axis=-1)
    cos = cos[:, None, :]
    sin = sin[:, None, :]
    return jnp.concatenate([x1 * cos - x2 * sin, x1 * sin + x2 * cos], axis=-1)

def rope_2d(x, tables):
    cos_r, sin_r, cos_c, sin_c = tables
    xr, xc = jnp.split(x.astype(jnp.float32), 2, axis=-1)
    out = jnp.concatenate([rotate_axis(xr, cos_r, sin_r), rotate_axis(xc, cos_c, sin_c)], axis=-1)
    return out.astype(x.dtype)

def swiglu(h, w_in, w_out):
    gate, up = jnp.split(h @ w_in, 2, axis=-1)
    return (jax.nn.silu(gate) * up) @ w_out

def windowed_gqa_sink(h_x, h_c, w_qkv, q_gain, k_gain, sink, w_o, need_ctx_out):
    B, S, _ = h_x.shape
    L = h_c.shape[1]
    nb = S // ATTN_BLOCK
    band = ATTN_BLOCK + 2 * WINDOW
    scale = HEAD_DIM ** -0.5
    qd = N_HEADS * HEAD_DIM
    kvd = N_KV_HEADS * HEAD_DIM
    tables = rope_tables(S, HEAD_DIM)
    sink_g = sink.astype(jnp.float32).reshape(N_KV_HEADS, GQA_GROUP)[None, :, :, None, None]

    q_x, k_x, v_x = jnp.split(h_x @ w_qkv, [qd, qd + kvd], axis=-1)
    q_x = rope_2d(rms_norm(q_x.reshape(B, S, N_HEADS, HEAD_DIM), q_gain), tables)
    q_x = q_x.reshape(B, S, N_KV_HEADS, GQA_GROUP, HEAD_DIM)
    k_x = rope_2d(rms_norm(k_x.reshape(B, S, N_KV_HEADS, HEAD_DIM), k_gain), tables)
    v_x = v_x.reshape(B, S, N_KV_HEADS, HEAD_DIM)
    k_c, v_c = jnp.split(h_c @ w_qkv[:, qd:], 2, axis=-1)
    k_c = rms_norm(k_c.reshape(B, L, N_KV_HEADS, HEAD_DIM), k_gain)
    v_c = v_c.reshape(B, L, N_KV_HEADS, HEAD_DIM)

    pad = ((0, 0), (WINDOW, WINDOW), (0, 0), (0, 0))
    k_pad = jnp.pad(k_x, pad)
    v_pad = jnp.pad(v_x, pad)
    r_idx = jnp.arange(ATTN_BLOCK, dtype=jnp.int32)[:, None]
    n_idx = jnp.arange(band, dtype=jnp.int32)[None, :]
    in_window = (n_idx >= r_idx) & (n_idx - r_idx <= 2 * WINDOW)

    def block(b):
        start = b * ATTN_BLOCK
        qb = lax.dynamic_slice_in_dim(q_x, start, ATTN_BLOCK, axis=1)
        kb = lax.dynamic_slice_in_dim(k_pad, start, band, axis=1)
        vb = lax.dynamic_slice_in_dim(v_pad, start, band, axis=1)
        key_pos = start - WINDOW + n_idx
        valid = in_window & (key_pos >= 0) & (key_pos < S)
        s_ctx = jnp.einsum('bqkgd,bnkd->bkgqn', qb, k_c, preferred_element_type=jnp.float32) * scale
        s_loc = jnp.einsum('bqkgd,bnkd->bkgqn', qb, kb, preferred_element_type=jnp.float32) * scale
        s_loc = jnp.where(valid, s_loc, NEG_INF)
        sink_col = jnp.broadcast_to(sink_g, s_ctx.shape[:-1] + (1,))
        p = jax.nn.softmax(jnp.concatenate([s_ctx, s_loc, sink_col], axis=-1), axis=-1).astype(vb.dtype)
        return (jnp.einsum('bkgqn,bnkd->bqkgd', p[..., :L], v_c)
                + jnp.einsum('bkgqn,bnkd->bqkgd', p[..., L:L + band], vb))

    o_x = jnp.moveaxis(lax.map(block, jnp.arange(nb, dtype=jnp.int32)), 0, 1).reshape(B, S, qd)
    out_x = o_x @ w_o

    out_c = None
    if need_ctx_out:
        q_c = rms_norm((h_c @ w_qkv[:, :qd]).reshape(B, L, N_HEADS, HEAD_DIM), q_gain)
        q_c = q_c.reshape(B, L, N_KV_HEADS, GQA_GROUP, HEAD_DIM)
        s_c = jnp.einsum('bqkgd,bnkd->bkgqn', q_c, k_c, preferred_element_type=jnp.float32) * scale
        sink_col = jnp.broadcast_to(sink_g, s_c.shape[:-1] + (1,))
        p_c = jax.nn.softmax(jnp.concatenate([s_c, sink_col], axis=-1), axis=-1).astype(v_c.dtype)
        o_c = jnp.einsum('bkgqn,bnkd->bqkgd', p_c[..., :L], v_c)
        out_c = o_c.reshape(B, L, qd) @ w_o
    return out_c, out_x

def retention_chunked(q, k, v, log_gamma, state0):
    B, T, H, _ = q.shape
    nc = T // RET_CHUNK
    pos = jnp.arange(RET_CHUNK, dtype=jnp.float32)
    diff = pos[:, None] - pos[None, :]
    intra = jnp.where(diff >= 0, jnp.exp(log_gamma[:, None, None] * jnp.maximum(diff, 0.0)), 0.0)
    q_decay = jnp.exp(log_gamma[None, :] * (pos + 1.0)[:, None])[None, :, :, None]
    k_decay = jnp.exp(log_gamma[None, :] * (RET_CHUNK - 1.0 - pos)[:, None])[None, :, :, None]
    chunk_decay = jnp.exp(log_gamma * RET_CHUNK)[None, :, None, None]

    def to_chunks(a):
        return jnp.moveaxis(a.reshape(B, nc, RET_CHUNK, H, a.shape[-1]), 1, 0)

    def step(state, inp):
        qc, kc, vc = inp
        scores = jnp.einsum('bnhd,bmhd->bhnm', qc, kc) * intra
        inner = jnp.einsum('bhnm,bmhe->bnhe', scores, vc)
        cross = jnp.einsum('bnhd,bhde->bnhe', qc, state) * q_decay
        new_state = state * chunk_decay + jnp.einsum('bmhd,bmhe->bhde', kc * k_decay, vc)
        return new_state, inner + cross

    state, out = lax.scan(step, state0, (to_chunks(q), to_chunks(k), to_chunks(v)))
    return jnp.moveaxis(out, 0, 1).reshape(B, T, H, v.shape[-1]), state

def retention_final_state(k, v, log_gamma):
    T = k.shape[1]
    pos = jnp.arange(T, dtype=jnp.float32)
    decay = jnp.exp(log_gamma[None, :] * (T - 1.0 - pos)[:, None])[None, :, :, None]
    return jnp.einsum('bthd,bthe->bhde', k * decay, v)

def bidir_retention(h_x, h_c, w_qkvg, decay_logit, gn_gain, w_o, need_ctx_out):
    B, S, _ = h_x.shape
    L = h_c.shape[1]
    qk = RET_HEADS * RET_QK_DIM
    f32 = jnp.float32
    tables = rope_tables(S, RET_QK_DIM)
    log_g = jax.nn.log_sigmoid(decay_logit.astype(f32))
    k_scale = RET_QK_DIM ** -0.5

    q_x, k_x, v_x, g_x = jnp.split(h_x @ w_qkvg, [qk, 2 * qk, 2 * qk + RET_VWIDTH], axis=-1)
    q_x = rope_2d(q_x.reshape(B, S, RET_HEADS, RET_QK_DIM), tables).astype(f32)
    k_x = rope_2d(k_x.reshape(B, S, RET_HEADS, RET_QK_DIM), tables).astype(f32) * k_scale
    v_x = v_x.reshape(B, S, RET_HEADS, RET_V_DIM).astype(f32)
    k_c, v_c = jnp.split(h_c @ w_qkvg[:, qk:2 * qk + RET_VWIDTH], [qk], axis=-1)
    k_c = k_c.reshape(B, L, RET_HEADS, RET_QK_DIM).astype(f32) * k_scale
    v_c = v_c.reshape(B, L, RET_HEADS, RET_V_DIM).astype(f32)

    def flip(a):
        return jnp.flip(a, axis=1)

    def gated_out(o, g):
        mu = jnp.mean(o, axis=-1, keepdims=True)
        var = jnp.mean(jnp.square(o - mu), axis=-1, keepdims=True)
        y = ((o - mu) * lax.rsqrt(var + EPS)).reshape(o.shape[0], o.shape[1], RET_VWIDTH) * gn_gain.astype(f32)
        return (jax.nn.silu(g) * y.astype(g.dtype)) @ w_o

    out_c = None
    if need_ctx_out:
        q_c = (h_c @ w_qkvg[:, :qk]).reshape(B, L, RET_HEADS, RET_QK_DIM).astype(f32)
        g_c = h_c @ w_qkvg[:, 2 * qk + RET_VWIDTH:]
        zero_state = jnp.zeros((B, RET_HEADS, RET_QK_DIM, RET_V_DIM), f32)
        oc_f, state_f = retention_chunked(q_c, k_c, v_c, log_g[0], zero_state)
        oc_b, state_b = retention_chunked(flip(q_c), flip(k_c), flip(v_c), log_g[1], zero_state)
        out_c = gated_out(oc_f + flip(oc_b), g_c)
    else:
        state_f = retention_final_state(k_c, v_c, log_g[0])
        state_b = retention_final_state(flip(k_c), flip(v_c), log_g[1])

    ox_f, _ = retention_chunked(q_x, k_x, v_x, log_g[0], state_f)
    ox_b, _ = retention_chunked(flip(q_x), flip(k_x), flip(v_x), log_g[1], state_b)
    out_x = gated_out(ox_f + flip(ox_b), g_x)
    return out_c, out_x

def first_inputs(seed: int = 0) -> dict:
    key = jax.random.key(seed)
    ks = jax.random.split(key, 19)
    f32 = jnp.float32

    def nrm(k, shape, scale):
        return jax.random.normal(k, shape, f32) * scale

    gamma = 1.0 - 2.0 ** (-5.0 - np.arange(RET_HEADS))
    decay_init = jnp.asarray(np.log(gamma / (1.0 - gamma)), dtype=f32)
    return {
        'x': nrm(ks[0], (BATCH, SEQ, D_MODEL), 1.0),
        'c': nrm(ks[1], (BATCH, D_MODEL), 1.0),
        'ctx': nrm(ks[2], (BATCH, CTX_LEN, D_MODEL), 1.0),
        'c_ctx': nrm(ks[3], (D_MODEL,), 1.0),
        'ada_w': nrm(ks[4], (DEPTH, D_MODEL, 6 * D_MODEL), 0.5 * D_MODEL ** -0.5),
        'ada_b': nrm(ks[5], (DEPTH, 6 * D_MODEL), 0.02),
        'norm1_g': 1.0 + nrm(ks[6], (DEPTH, D_MODEL), 0.02),
        'norm2_g': 1.0 + nrm(ks[7], (DEPTH, D_MODEL), 0.02),
        'ffn_w_in': nrm(ks[8], (DEPTH, D_MODEL, 2 * D_FF), D_MODEL ** -0.5),
        'ffn_w_out': nrm(ks[9], (DEPTH, D_FF, D_MODEL), D_FF ** -0.5),
        'attn_w_qkv': nrm(ks[10], (N_ATTN_LAYERS, D_MODEL, ATTN_PROJ), D_MODEL ** -0.5),
        'attn_q_norm': 1.0 + nrm(ks[11], (N_ATTN_LAYERS, HEAD_DIM), 0.02),
        'attn_k_norm': 1.0 + nrm(ks[12], (N_ATTN_LAYERS, HEAD_DIM), 0.02),
        'attn_sink': nrm(ks[13], (N_ATTN_LAYERS, N_HEADS), 0.5),
        'attn_w_o': nrm(ks[14], (N_ATTN_LAYERS, N_HEADS * HEAD_DIM, D_MODEL), (N_HEADS * HEAD_DIM) ** -0.5),
        'ret_w_qkvg': nrm(ks[15], (N_RET_LAYERS, D_MODEL, RET_PROJ), D_MODEL ** -0.5),
        'ret_decay_logit': decay_init[None, None, :] + nrm(ks[16], (N_RET_LAYERS, 2, RET_HEADS), 0.01),
        'ret_gn_g': 1.0 + nrm(ks[17], (N_RET_LAYERS, RET_VWIDTH), 0.02),
        'ret_w_o': nrm(ks[18], (N_RET_LAYERS, RET_VWIDTH, D_MODEL), RET_VWIDTH ** -0.5),
    }

def first_block(x, c, ctx, c_ctx, ada_w, ada_b, norm1_g, norm2_g, ffn_w_in, ffn_w_out,
              attn_w_qkv, attn_q_norm, attn_k_norm, attn_sink, attn_w_o,
              ret_w_qkvg, ret_decay_logit, ret_gn_g, ret_w_o):
    c_act = jax.nn.silu(c)[:, None, :]
    cc_act = jax.nn.silu(c_ctx)[None, None, :]
    y_ctx = ctx
    for i in range(DEPTH):
        need_ctx_out = i < DEPTH - 1
        mx = jnp.split(c_act @ ada_w[i] + ada_b[i], 6, axis=-1)
        mc = jnp.split(cc_act @ ada_w[i] + ada_b[i], 6, axis=-1)
        h_x = modulate(rms_norm(x, norm1_g[i]), mx[0], mx[1])
        h_c = modulate(rms_norm(y_ctx, norm1_g[i]), mc[0], mc[1])
        j = i // N_MIXERS
        if i % N_MIXERS == 0:
            out_c, out_x = windowed_gqa_sink(h_x, h_c, attn_w_qkv[j], attn_q_norm[j], attn_k_norm[j],
                                             attn_sink[j], attn_w_o[j], need_ctx_out)
        else:
            out_c, out_x = bidir_retention(h_x, h_c, ret_w_qkvg[j], ret_decay_logit[j], ret_gn_g[j],
                                           ret_w_o[j], need_ctx_out)
        x = x + mx[2] * out_x
        x = x + mx[5] * swiglu(modulate(rms_norm(x, norm2_g[i]), mx[3], mx[4]), ffn_w_in[i], ffn_w_out[i])
        if need_ctx_out:
            y_ctx = y_ctx + mc[2] * out_c
            y_ctx = y_ctx + mc[5] * swiglu(modulate(rms_norm(y_ctx, norm2_g[i]), mc[3], mc[4]),
                                           ffn_w_in[i], ffn_w_out[i])
    return x


N_GROUPS = 4
GROUP_W = D_MODEL // N_GROUPS
HEADS = 4
HEAD_DIM_2 = GROUP_W // HEADS
CHUNK = 128
DIFF_QK = HEAD_DIM_2 // 2
ROT_HALF = DIFF_QK // 2
ROPE_THETA = 10000.0
Q_BLOCK = 128
D_FF_2 = 2816
G_AU, G_AV, G_BX, G_BB, G_BC, G_CF, G_DQ, G_DK, G_DV = range(9)
IN_COLS = 9 * GROUP_W
KV_COL0 = G_DK * GROUP_W


def rmsnorm(x, g=None):
    xf = x.astype(jnp.float32)
    y = xf * lax.rsqrt(jnp.mean(xf * xf, axis=-1, keepdims=True) + EPS)
    if g is not None:
        y = y * g.astype(jnp.float32)
    return y.astype(x.dtype)

def adaln_params(cvec, w_ada, b_ada):
    m = jax.nn.silu(cvec) @ w_ada + b_ada
    return jnp.split(m, 6, axis=-1)

def modulate_2(h, shift, scale):
    return h * (1 + scale) + shift

def group(z, i):
    return z[..., i * GROUP_W:(i + 1) * GROUP_W]

def dwconv3(x, w):
    xp = jnp.pad(x, ((0, 0), (1, 1), (0, 0)))
    return xp[:, :-2] * w[0] + xp[:, 1:-1] * w[1] + xp[:, 2:] * w[2]

def mixer_a(z, ws, bs):
    B, N, _ = z.shape
    u = jax.nn.gelu(group(z, G_AU))
    v = rmsnorm(jax.nn.gelu(group(z, G_AV)).reshape(B, N, HEADS, HEAD_DIM_2))
    v = v.reshape(B, N // CHUNK, CHUNK, HEADS, HEAD_DIM_2)
    mixed = jnp.einsum('hpq,bcqhd->bcphd', ws, v) + bs.T[:, :, None]
    return u * mixed.reshape(B, N, GROUP_W)

def mixer_b(z, w):
    return group(z, G_BB) * dwconv3(group(z, G_BC) * group(z, G_BX), w)

def mixer_c(z):
    B, N, _ = z.shape
    f = group(z, G_CF).reshape(B, N, HEADS, HEAD_DIM_2).astype(jnp.float32)
    F = jnp.fft.fft2(f, axes=(1, 3), norm='ortho').real
    return F.astype(z.dtype).reshape(B, N, GROUP_W)

def apply_rope_2d(t, ang_r, ang_c):
    def rot(u, ang):
        cos = jnp.cos(ang)[None, :, None, None, :].astype(u.dtype)
        sin = jnp.sin(ang)[None, :, None, None, :].astype(u.dtype)
        u1, u2 = u[..., :ROT_HALF // 2], u[..., ROT_HALF // 2:]
        return jnp.concatenate([u1 * cos - u2 * sin, u2 * cos + u1 * sin], axis=-1)
    return jnp.concatenate([rot(t[..., :ROT_HALF], ang_r), rot(t[..., ROT_HALF:], ang_c)], axis=-1)

def diff_attend(q, k, v, lam):
    s = jnp.einsum('bqhmd,bkhmd->bhmqk', q, k).astype(jnp.float32) * (DIFF_QK ** -0.5)
    p = jax.nn.softmax(s, axis=-1)
    a = p[:, :, 0] - lam * p[:, :, 1]
    return jnp.einsum('bhqk,bkhd->bqhd', a.astype(v.dtype), v)

def diff_out(o, g, lam_init):
    B, N = o.shape[0], o.shape[1]
    return (rmsnorm(o, g) * (1 - lam_init)).reshape(B, N, GROUP_W)

def conv_ffn(h, w_up, conv_w, w_down):
    up = h @ w_up
    a, b = up[..., :D_FF_2], up[..., D_FF_2:]
    return (jax.nn.silu(dwconv3(a, conv_w)) * b) @ w_down

def trunk_layer(x, xc, c, c_ctx, ang_r, ang_c, layer_idx, ctx_out,
                w_ada, b_ada, g1, g2, w_in, gm_ws, gm_bs, sc_w,
                lq1, lk1, lq2, lk2, subln_g, w_out, w_up, ffn_conv, w_down):
    B, N, _ = x.shape
    L = xc.shape[1]
    sh1, sc1, gt1, sh2, sc2, gt2 = [m[:, None, :] for m in adaln_params(c, w_ada, b_ada)]
    shc1, scc1, gtc1, shc2, scc2, gtc2 = adaln_params(c_ctx, w_ada, b_ada)
    lam_init = 0.8 - 0.6 * math.exp(-0.3 * layer_idx)
    f32 = jnp.float32
    lam = (jnp.exp(jnp.sum(lq1.astype(f32) * lk1.astype(f32)))
           - jnp.exp(jnp.sum(lq2.astype(f32) * lk2.astype(f32))) + lam_init)

    h = modulate_2(rmsnorm(x, g1), sh1, sc1)
    hc = modulate_2(rmsnorm(xc, g1), shc1, scc1)
    z = h @ w_in
    zc_kv = hc @ w_in[:, KV_COL0:]
    kc = zc_kv[..., :GROUP_W].reshape(B, L, HEADS, 2, DIFF_QK)
    vc = zc_kv[..., GROUP_W:].reshape(B, L, HEADS, HEAD_DIM_2)

    q = apply_rope_2d(group(z, G_DQ).reshape(B, N, HEADS, 2, DIFF_QK), ang_r, ang_c)
    k = apply_rope_2d(group(z, G_DK).reshape(B, N, HEADS, 2, DIFF_QK), ang_r, ang_c)
    v = group(z, G_DV).reshape(B, N, HEADS, HEAD_DIM_2)
    k_all = jnp.concatenate([kc, k], axis=1)
    v_all = jnp.concatenate([vc, v], axis=1)
    qb = q.reshape(B, N // Q_BLOCK, Q_BLOCK, HEADS, 2, DIFF_QK).swapaxes(0, 1)
    o = lax.map(lambda qi: diff_attend(qi, k_all, v_all, lam), qb)
    o = o.swapaxes(0, 1).reshape(B, N, HEADS, HEAD_DIM_2)

    mix = jnp.concatenate([mixer_a(z, gm_ws, gm_bs), mixer_b(z, sc_w), mixer_c(z),
                           diff_out(o, subln_g, lam_init)], axis=-1)
    x = x + gt1 * (mix @ w_out)
    x = x + gt2 * conv_ffn(modulate_2(rmsnorm(x, g2), sh2, sc2), w_up, ffn_conv, w_down)
    if not ctx_out:
        return x, None

    zc = hc @ w_in[:, :KV_COL0]
    qc = group(zc, G_DQ).reshape(B, L, HEADS, 2, DIFF_QK)
    oc = diff_attend(qc, kc, vc, lam)
    mixc = jnp.concatenate([mixer_a(zc, gm_ws, gm_bs), mixer_b(zc, sc_w), mixer_c(zc),
                            diff_out(oc, subln_g, lam_init)], axis=-1)
    xc = xc + gtc1 * (mixc @ w_out)
    xc = xc + gtc2 * conv_ffn(modulate_2(rmsnorm(xc, g2), shc2, scc2), w_up, ffn_conv, w_down)
    return x, xc

def second_inputs(seed: int = 0) -> dict:
    key = jax.random.key(seed)
    ks = jax.random.split(key, 24)
    D = D_MODEL

    def nrm(k, shape, scale):
        return jax.random.normal(k, shape, jnp.float32) * scale

    return {
        'x': nrm(ks[0], (BATCH, SEQ, D), 1.0),
        'c': nrm(ks[1], (BATCH, D), 1.0),
        'ctx': nrm(ks[2], (BATCH, CTX_LEN, D), 1.0),
        'c_ctx': nrm(ks[3], (D,), 1.0),
        'w_ada': nrm(ks[4], (DEPTH, D, 6 * D), 0.5 * D ** -0.5),
        'b_ada': nrm(ks[5], (DEPTH, 6 * D), 0.02),
        'norm1_g': 1.0 + nrm(ks[6], (DEPTH, D), 0.02),
        'norm2_g': 1.0 + nrm(ks[7], (DEPTH, D), 0.02),
        'w_in': nrm(ks[8], (DEPTH, D, IN_COLS), D ** -0.5),
        'gmlp_ws': nrm(ks[9], (DEPTH, HEADS, CHUNK, CHUNK), CHUNK ** -0.5),
        'gmlp_bs': 1.0 + nrm(ks[10], (DEPTH, HEADS, CHUNK), 0.02),
        'sconv_w': nrm(ks[11], (DEPTH, 3, GROUP_W), 3 ** -0.5),
        'lambda_q1': nrm(ks[12], (DEPTH, DIFF_QK), 0.1),
        'lambda_k1': nrm(ks[13], (DEPTH, DIFF_QK), 0.1),
        'lambda_q2': nrm(ks[14], (DEPTH, DIFF_QK), 0.1),
        'lambda_k2': nrm(ks[15], (DEPTH, DIFF_QK), 0.1),
        'subln_g': 1.0 + nrm(ks[16], (DEPTH, HEAD_DIM_2), 0.02),
        'w_out': nrm(ks[17], (DEPTH, D, D), D ** -0.5),
        'ffn_w_up': nrm(ks[18], (DEPTH, D, 2 * D_FF_2), D ** -0.5),
        'ffn_conv_w': nrm(ks[19], (DEPTH, 3, D_FF_2), 3 ** -0.5),
        'ffn_w_down': nrm(ks[20], (DEPTH, D_FF_2, D), D_FF_2 ** -0.5),
        'final_g': 1.0 + nrm(ks[21], (D,), 0.02),
    }

def second_block(x, c, ctx, c_ctx, w_ada, b_ada, norm1_g, norm2_g, w_in, gmlp_ws, gmlp_bs,
              sconv_w, lambda_q1, lambda_k1, lambda_q2, lambda_k2, subln_g, w_out,
              ffn_w_up, ffn_conv_w, ffn_w_down, final_g):
    N = x.shape[1]
    ROWS = N // GRID_W
    row = jnp.broadcast_to(jnp.arange(ROWS, dtype=jnp.float32)[:, None], (ROWS, GRID_W)).reshape(-1)
    col = jnp.broadcast_to(jnp.arange(GRID_W, dtype=jnp.float32)[None, :], (ROWS, GRID_W)).reshape(-1)
    inv_freq = ROPE_THETA ** (-jnp.arange(0, ROT_HALF, 2, dtype=jnp.float32) / ROT_HALF)
    ang_r = row[:, None] * inv_freq
    ang_c = col[:, None] * inv_freq
    xc = ctx
    for l in range(DEPTH):
        x, xc = trunk_layer(
            x, xc, c, c_ctx, ang_r, ang_c, l, l < DEPTH - 1,
            w_ada[l], b_ada[l], norm1_g[l], norm2_g[l], w_in[l], gmlp_ws[l], gmlp_bs[l],
            sconv_w[l], lambda_q1[l], lambda_k1[l], lambda_q2[l], lambda_k2[l], subln_g[l],
            w_out[l], ffn_w_up[l], ffn_conv_w[l], ffn_w_down[l])
    return rmsnorm(x, final_g)


def setup_inputs(seed=0):
    out = dict(first_inputs(seed))
    for name, value in second_inputs(seed + 1).items():
        if name != "x":
            out[name + "_2"] = value
    return out


def reference(
    x, c, ctx, c_ctx, ada_w, ada_b, norm1_g, norm2_g, ffn_w_in, ffn_w_out, attn_w_qkv,
    attn_q_norm, attn_k_norm, attn_sink, attn_w_o, ret_w_qkvg, ret_decay_logit, ret_gn_g,
    ret_w_o, c_2, ctx_2, c_ctx_2, w_ada_2, b_ada_2, norm1_g_2, norm2_g_2, w_in_2, gmlp_ws_2,
    gmlp_bs_2, sconv_w_2, lambda_q1_2, lambda_k1_2, lambda_q2_2, lambda_k2_2, subln_g_2,
    w_out_2, ffn_w_up_2, ffn_conv_w_2, ffn_w_down_2, final_g_2,
):
    x = first_block(
        x, c, ctx, c_ctx, ada_w, ada_b, norm1_g, norm2_g, ffn_w_in, ffn_w_out, attn_w_qkv,
        attn_q_norm, attn_k_norm, attn_sink, attn_w_o, ret_w_qkvg, ret_decay_logit, ret_gn_g,
        ret_w_o,
    )
    return second_block(
        x, c_2, ctx_2, c_ctx_2, w_ada_2, b_ada_2, norm1_g_2, norm2_g_2, w_in_2, gmlp_ws_2,
        gmlp_bs_2, sconv_w_2, lambda_q1_2, lambda_k1_2, lambda_q2_2, lambda_k2_2, subln_g_2,
        w_out_2, ffn_w_up_2, ffn_conv_w_2, ffn_w_down_2, final_g_2,
    )


_drawn_inputs = setup_inputs


def setup_inputs(seed=0):
    import zlib

    import numpy as np

    out = dict(_drawn_inputs(seed))
    spreads = {}
    factors = {'norm1_g': 6.986,
     'norm2_g': 5.839,
     'attn_q_norm': 8.0,
     'attn_k_norm': 8.0,
     'attn_sink': 8.0,
     'ret_gn_g': 8.0,
     'norm1_g_2': 5.331,
     'norm2_g_2': 26.606,
     'gmlp_bs_2': 64.0,
     'lambda_q1_2': 41.89,
     'lambda_k1_2': 5.937,
     'lambda_q2_2': 119.643,
     'lambda_k2_2': 8.0,
     'subln_g_2': 200.0,
     'final_g_2': 23.787,
     'gmlp_ws_2': 2.704}
    for name, (base, spread) in spreads.items():
        noise = np.random.default_rng([zlib.crc32(name.encode()), seed]).standard_normal(out[name].shape)
        drawn = base * np.exp(spread * noise) if base else spread * noise
        out[name] = jnp.asarray(drawn.astype(out[name].dtype))
    for name, factor in factors.items():
        out[name] = (out[name] * factor).astype(out[name].dtype)
    return out
```

```python
from contextlib import ExitStack, contextmanager

import concourse.bass as bass
from concourse import mybir
import numpy as np

ALU = mybir.AluOpType
ACT = mybir.ActivationFunctionType
F32 = mybir.dt.float32
F32R = mybir.dt.float32r
BF16 = mybir.dt.bfloat16
AX = mybir.AxisListType.X

P = 128
D = 1024
KT = D // P
S = 512
L = 256
T = S + L
FF = 2816
FT = FF // P
CH = 2
FC = FT // CH
NV = 6 * D // P
EPS = 1e-6
START = 96
UNIT = KT * P
DUNIT = FC * P
ALL = ((0, S, 0), (S, T, 1))
IMG = ((0, S, 0),)


class Count:

    def __init__(self, sem, value, loop):
        self.sem, self.value, self.loop = sem, value, loop


class Chip:

    def __init__(self, nc, ctx, book, dry):
        self.nc, self.ctx, self.book, self.dry = nc, ctx, book, dry
        self.sems, self.cnt, self.loop, self.last, self.past = {}, {}, None, {}, {}

    def sem(self, name):
        if name not in self.sems:
            self.sems[name] = self.ctx.enter_context(self.nc.semaphore(name))
            self.cnt[name] = 0
        return self.sems[name]

    def inc(self, ins, sem, name=None, by=1):
        ins.then_inc(self.sem(sem), by)
        self.cnt[sem] += by
        c = Count(sem, self.cnt[sem], self.loop)
        if name:
            self.name(c, name)
        return c

    def name(self, c, name):
        self.last[name] = c
        if self.loop:
            self.book[self.loop["name"]]["at"][name] = (c.sem, c.value - self.loop["base"].get(c.sem, 0))

    def now(self, sem):
        self.sem(sem)
        return Count(sem, self.cnt[sem], self.loop)

    def prev(self, name):
        lp = self.loop
        sem, at = self.book[lp["name"]]["at"].get(name, ("dve", 1))
        self.sem(sem)
        return Count(sem, lp["base"].get(sem, 0) + at - self.stride(sem), lp)

    def before(self, name):
        c = self.last.get(name)
        if self.loop is None or c is not None and c.loop is self.loop:
            return c
        return self.prev(name)

    def stride(self, sem):
        return self.book[self.loop["name"]]["step"].get(sem, 1)

    def wait(self, eng, *counts):
        top = {}
        for c in counts:
            if c is None:
                continue
            inside, v = c.loop is not None and c.loop is self.loop, c.value
            step = self.book[c.loop["name"]]["step"].get(c.sem, 0 if not self.dry else 1) if c.loop else 0
            if c.loop and not inside:
                v += (c.loop["n"] - 1) * step
            key = (c.sem, inside)
            if key not in top or v > top[key][0]:
                top[key] = (v, step if inside else 0)
        for key, (v, step) in top.items():
            past = (str(eng.engine), key)
            if v <= 0 and not step or self.past.get(past, 0) >= v > 0:
                continue
            self.past[past] = v
            assert v >= 1 or self.dry, (self.loop["name"], key, v)
            eng.wait_ge(self.sem(key[0]), self.loop["i"] * step + v if step else v)

    @contextmanager
    def fori(self, name, n):
        rec = self.book.setdefault(name, {"step": {}, "at": {}})
        base = dict(self.cnt)
        with self.nc.Fori(0, n) as i:
            self.past = {}
            self.loop = {"name": name, "base": base, "i": i, "n": n}
            yield i
            steps = {s: v - base.get(s, 0) for s, v in self.cnt.items() if v != base.get(s, 0)}
            assert self.dry or rec["step"] == steps, (name, rec["step"], steps)
            rec["step"] = steps
            self.loop, self.past = None, {}
        for s, v in steps.items():
            self.cnt[s] = base.get(s, 0) + n * v

    def barrier(self, *engs):
        for e in engs or (self.nc.tensor, self.nc.scalar, self.nc.vector, self.nc.gpsimd):
            for s in ("pe", "act", "dve", "pool", "norm_act", "norm_dve"):
                if s in self.cnt and self.cnt[s]:
                    self.wait(e, self.now(s))


def build(nc, dram, out, book, dry):
    with ExitStack() as ctx:
        c = Chip(nc, ctx, book, dry)
        PE, AC, VE, PO, SP = nc.tensor, nc.scalar, nc.vector, nc.gpsimd, nc.sync
        wait, inc = c.wait, c.inc
        for eng, name in ((PE, "pe"), (AC, "act"), (VE, "dve"), (PO, "pool")):
            eng.sem_inc(c.sem(name), START)
            c.cnt[name] = START

        def sb(name, shape, dt=F32, stack=ctx):
            return stack.enter_context(nc.sbuf_tensor(name, shape, dt))

        X = sb("X", [P, KT, T])
        HH = sb("HH", [P, KT, T], F32R)
        HL = sb("HL", [P, KT, T], F32R)
        WR = [sb(f"WR{s}", [P, DUNIT]) for s in range(2)]
        WH = [sb(f"WH{s}", [P, DUNIT], F32R) for s in range(2)]
        WL = [sb(f"WL{s}", [P, DUNIT], F32R) for s in range(2)]
        MOD = sb("MOD", [P, 4, NV, 2])
        SCL = sb("SCL", [P, 4, 2, KT, 2])
        CAC = sb("CAC", [P, 2, KT, 32])
        CIN = sb("CIN", [P, 2, KT, 2])
        ADB = sb("ADB", [P, 4, NV])
        GN = sb("GN", [P, 4, 2, KT])
        SEL = sb("SEL", [P, 2])
        ONE = sb("ONE", [P, P])
        EPSC = sb("EPSC", [P, 1])
        PS = [ctx.enter_context(nc.psum_tensor(f"PS{b}", [P, 1024], F32)) for b in range(4)]

        def lanes(pair, n):
            return PS[pair][:, 0:n]

        def refill_hi(slot, src, n):
            wait(SP, c.now(f"lo{slot}"))
            inc(SP.dma_start(WR[slot][:, 0:n], src), f"ld{slot}", by=16)
            wait(AC, c.now(f"ld{slot}"), c.now(f"mm{slot}"))
            inc(AC.activation(WH[slot][:, 0:n], WR[slot][:, 0:n], ACT.Copy), f"hi{slot}")

        def refill_lo(slot, n):
            wait(VE, c.now(f"hi{slot}"))
            inc(VE.tensor_tensor(WL[slot][:, 0:n], WR[slot][:, 0:n], WH[slot][:, 0:n].bitcast(F32), ALU.subtract),
                f"lo{slot}")

        def refill(slot, unit):
            if unit is not None:
                refill_hi(slot, *unit)
                refill_lo(slot, unit[1])

        def product(slot, dst, src, nk, segs, free=(), ready=()):
            wait(PE, c.now(f"lo{slot}"), *free)
            sh, sl = src
            n = 3 * nk
            i = 0
            for k in range(nk):
                wait(PE, *ready[k:k + 1])
                for w, h in ((WH, sh), (WH, sl), (WL, sh)):
                    for a, b, _ in segs:
                        m = PE.matmul(dst[:, a:b], w[slot][:, k * P:(k + 1) * P], h[:, k, a:b],
                                      start=(i == 0), stop=(i == n - 1))
                    i += 1
            return inc(m, f"mm{slot}")

        def rsqrt(dst, var, tmp, ready, name=None):
            wait(AC, ready)
            y = inc(AC.activation(dst, var, ACT.Abs_reciprocal_sqrt, bias=EPSC[:, 0:1]), "act")
            wait(AC, y)
            h = inc(AC.activation(tmp, dst, ACT.Square, scale=0.5 ** 0.5), "act")
            wait(VE, h)
            u = inc(VE.scalar_tensor_tensor(tmp, var, EPS, tmp, ALU.add, ALU.mult), "dve")
            wait(VE, u)
            return inc(VE.scalar_tensor_tensor(dst, tmp, 1.5, dst, ALU.subtract, ALU.mult, reverse0=True), "dve", name)

        def at(t, i, a, b):
            return t[:, i, a:b] if isinstance(i, int) else t[:, bass.ds(i, 1), a:b].rearrange("p k t -> p (k t)")

        def split(hi, lo, src, ready, name=None):
            wait(AC, ready)
            h = inc(AC.activation(hi, src, ACT.Copy), "act")
            wait(VE, h)
            return inc(VE.tensor_tensor(lo, src, hi.bitcast(F32), ALU.subtract), "dve", name)

        def product_rows(slot, unit_k, k0, width, tiles, dst, first, last, free=()):
            wait(PE, c.now(f"lo{slot}"), *free)
            for m in tiles:
                i = 0
                for k in range(unit_k):
                    for h, w in ((HH, WH), (HH, WL), (HL, WH)):
                        mm = PE.matmul(dst(m), h[:, k0 + k, m * P:(m + 1) * P], w[slot][:, k * width:(k + 1) * width],
                                       start=(first and i == 0), stop=(last and i == 3 * unit_k - 1))
                        i += 1
            return inc(mm, f"mm{slot}")

        def squares_start(n, wk):
            c.barrier(PO)
            inc(PO.memset(wk[2][:, 0:n], 0.0), "pool", "sq_add")

        def squares_add(k, half, n, wk, ready):
            wait(AC, ready, c.before(f"sq_add{half}") if c.loop else c.last.get(f"sq_add{half}"))
            sq = inc(AC.activation(wk[half][:, 0:n], at(X, k, 0, n), ACT.Square), "act", "sq")
            if not isinstance(k, int) or k < KT - 1:
                wait(PO, sq, c.before("sq_add"))
                a = inc(PO.tensor_tensor(wk[2][:, 0:n], wk[2][:, 0:n], wk[half][:, 0:n], ALU.add), "pool", "sq_add")
                c.name(a, f"sq_add{half}")

        def project(tag, l, gate, units, segs, nxt, wk, src=(HH, HL)):
            c.barrier()
            squares_start(segs[-1][1], wk)

            def tile(n, half, free, nx):
                o = product(half, PS[half], src, KT, segs, (free,))
                refill(half, nx)
                wait(VE, o)
                for a, b, j in segs:
                    gv = MOD[:, l, gate + n, j:j + 1] if isinstance(n, int) else MOD[:, l, bass.ds(n + gate, 1), j]
                    xx = at(X, n, a, b)
                    v = inc(VE.scalar_tensor_tensor(xx, PS[half][:, a:b], gv, xx, ALU.mult, ALU.add),
                            "dve", f"out_read{half}")
                squares_add(n, half, segs[-1][1], wk, v)

            with c.fori(f"proj{tag}", KT // 2 - 1) as i:
                for half in range(2):
                    tile(i * 2 + half, half, c.prev(f"out_read{half}"), (units(i * 2 + (half + 2)), UNIT))
            for half in range(2):
                tile(KT - 2 + half, half, c.last[f"out_read{half}"], nxt[half])

        loads = [(CIN, "cin"), (ADB, "adb"), (GN, "gn"), (SEL, "sel")]
        CW = sb("CW", [P, 2, FT, 3])
        inc(SP.dma_start(CW[:, :, :, :], dram["ffnconv"]), "small", by=16)
        for t, name in loads:
            ap = t[:, :] if len(t.shape) == 2 else t[:].rearrange(
                {3: "p a b -> p (a b)", 4: "p a b c -> p (a b c)"}[len(t.shape)])
            inc(SP.dma_start(ap, dram[name]), "small", by=16)
        inc(VE.memset(ONE[:, :], 1.0 / D), "dve")
        inc(VE.memset(EPSC[:, :], EPS), "dve")
        z = inc(VE.memset(CAC[:, :, :, :], 0.0), "dve")
        wait(AC, z, c.now("small"))
        cact = inc(AC.activation(CAC[:, :, :, 0:2], CIN[:, :, :, :], ACT.Silu), "act")

        NA = 6 * D // 512
        acc, tr = PS[3][:, 0:512], PS[3][:, 512:512 + 2 * NV]

        def ada_load(l, nb, half, buf, free):
            wait(SP, free)
            inc(SP.dma_start(buf[half], dram["ada"][(nb + l * NA) * 2 + half]), f"ada{half}", by=16)

        def ada_start(l, buf):
            for half in range(2):
                ada_load(l, 0, half, buf, None)

        def ada_sum(l, nb, buf):
            wait(PE, cact)
            for half in range(2):
                wait(PE, c.now(f"ada{half}"), c.before("adaev") if half == 0 else None)
                for q in range(4):
                    m = PE.matmul(acc[32 * q:32 * q + 32, :], CAC[:, l // 2, 4 * half + q, :], buf[half][:, q, :],
                                  start=(half == 0), stop=(half == 1))
                done = inc(m, "pe", f"adamm{half}")
            wait(AC, done, c.before("adatr"))
            inc(AC.activation(buf[2], acc, ACT.Copy), "act", "adaev")

        def ada_next(l, nb, buf):
            for half in range(2):
                ada_load(l, nb + 1, half, buf, c.last[f"adamm{half}"])

        def ada_turn(nb, buf):
            wait(PE, c.last["adaev"])
            for s in range(4):
                dst = tr[:, bass.ds(nb * 8 + 2 * s, 2)] if not isinstance(nb, int) else tr[:, nb * 8 + 2 * s:nb * 8 + 2 * s + 2]
                m = PE.matmul(dst, buf[2][:, s * P:(s + 1) * P], SEL[:, :], start=True, stop=True)
            inc(m, "pe", "adatr")

        def ada_finish(l, v0=0, v1=NV):
            wait(VE, c.last["adatr"], c.now("small"))
            for j in range(2):
                v = inc(VE.tensor_tensor(MOD[:, l, v0:v1, j], tr.rearrange("p (v j) -> p v j", j=2)[:, v0:v1, j],
                                         ADB[:, l, v0:v1], ALU.add), "dve")
            wait(VE, v)
            for which in range(2):
                if v0 <= 24 * which + 8 and 24 * which + 16 <= v1:
                    for j in range(2):
                        inc(VE.scalar_tensor_tensor(SCL[:, l, which, :, j],
                                                    MOD[:, l, 24 * which + 8:24 * which + 16, j], 1.0,
                                                    GN[:, l, which, :], ALU.add, ALU.mult), "dve")

        def mean_square(n, segs, wk, summed):
            if summed:
                wait(PE, c.last["sq"], c.last["sq_add"])
                for i, t in enumerate((wk[2], wk[1])):
                    for a, b, _ in segs:
                        m = PE.matmul(PS[2][:, a:b], ONE[:, :], t[:, a:b], start=(i == 0), stop=(i == 1))
                return inc(m, "pe")
            pe = [None, None]
            for k in range(KT):
                wait(AC, pe[k % 2])
                sq = inc(AC.activation(wk[k % 2][:, 0:n], X[:, k, 0:n], ACT.Square), "act")
                wait(PE, sq)
                for a, b, _ in segs:
                    m = PE.matmul(PS[2][:, a:b], ONE[:, :], wk[k % 2][:, a:b], start=(k == 0), stop=(k == KT - 1))
                pe[k % 2] = inc(m, "pe")
            return pe[1]

        def norm(tag, l, which, segs, wk, summed):
            n = segs[-1][1]
            with ExitStack() as st:
                TT = [sb(f"TT{tag}{i}", [P, T], F32, st) for i in range(5)]
                RS = sb(f"RS{tag}", [P, T], F32, st)
                RI = sb(f"RI{tag}", [P, T], F32, st)
                c.barrier()
                if tag == "0a":
                    wait(AC, c.now("xin"))
                ri = rsqrt(RI[:, 0:n], PS[2][:, 0:n], RS[:, 0:n], mean_square(n, segs, wk, summed))
                wait(VE, ri)
                wait(PO, ri)
                pool = (3, 6)
                whole = {}
                for k in pool:
                    t = TT[3 + pool.index(k)]
                    p1 = inc(PO.tensor_tensor(t[:, 0:n], X[:, k, 0:n], RI[:, 0:n], ALU.mult), "pool")
                    wait(PO, p1)
                    for a, b, j in segs:
                        whole[k] = inc(PO.tensor_scalar(t[:, a:b], t[:, a:b], SCL[:, l, which, k, j:j + 1],
                                                        MOD[:, l, 24 * which + k, j:j + 1], ALU.mult, ALU.add), "pool")
                done, hi, slot = [None] * KT, [None] * KT, {}

                def rest(k):
                    wait(VE, hi[k])
                    if k in pool:
                        t = TT[3 + pool.index(k)]
                        done[k] = inc(VE.tensor_tensor(HL[:, k, 0:n], t[:, 0:n], HH[:, k, 0:n].bitcast(F32),
                                                       ALU.subtract), "norm_dve")
                        return
                    for a, b, j in segs:
                        done[k] = inc(VE.scalar_tensor_tensor(HL[:, k, a:b], slot[k][:, a:b], MOD[:, l, 24 * which + k, j:j + 1],
                                                              HH[:, k, a:b].bitcast(F32), ALU.add, ALU.subtract), "norm_dve")

                for k in range(KT):
                    if k in pool:
                        wait(AC, whole[k])
                        hi[k] = inc(AC.activation(HH[:, k, 0:n], TT[3 + pool.index(k)][:, 0:n], ACT.Copy), "norm_act")
                    else:
                        i = len(slot)
                        slot[k] = TT[i % 3]
                        wait(VE, done[k - 3] if i >= 3 else None, done[k - 4] if i >= 3 else None)
                        for a, b, j in segs:
                            v = inc(VE.scalar_tensor_tensor(slot[k][:, a:b], X[:, k, a:b], SCL[:, l, which, k, j:j + 1],
                                                            RI[:, a:b], ALU.mult, ALU.mult), "norm_dve")
                        wait(AC, v)
                        for a, b, j in segs:
                            hi[k] = inc(AC.activation(HH[:, k, a:b], slot[k][:, a:b], ACT.Identity,
                                                      bias=MOD[:, l, 24 * which + k, j:j + 1]), "norm_act")
                    if k:
                        rest(k - 1)
                rest(KT - 1)
                return done

        def ffn(tag, l, segs, nxt, wk, ready, conv=None, ada=None):
            n = segs[-1][1]
            win, wdn = dram[f"win{l}"], dram[f"wdn{l}"]

            def win_unit(j, half):
                return win[j * 2 + half], UNIT

            def down_unit(ch, m):
                return wdn[m + ch * KT], DUNIT

            with ExitStack() as st:
                DH = sb(f"DH{tag}", [P, FC, T], F32R, st)
                DL = sb(f"DL{tag}", [P, FC, T], F32R, st)
                SG, HF = wk[0:2]
                buf = [sb(f"AR{tag}_{i}", [P, 4, 512], F32, st) for i in range(2)] + [sb(f"EV{tag}_", [P, 512], F32, st)]
                buf = (buf[0][:, :, :], buf[1][:, :, :], buf[2][:, :])
                c.barrier(AC, VE, PO)
                if ada is not None:
                    ada_start(ada, buf)

                def hidden(j, jj, ev, free_up, sg_free, hf_free, nx, ready=(), part=None):
                    g = product(0, PS[0], (HH, HL), KT, segs, (ev,), ready)
                    if part is not None and ada is not None:
                        ada_sum(ada, part, buf)
                    u = product(1, PS[1], (HH, HL), KT, segs, (free_up,))
                    if part is not None and ada is not None:
                        ada_turn(part, buf)
                    wait(AC, g, sg_free)
                    if conv is None:
                        sg = inc(AC.activation(SG[:, 0:n], PS[0][:, 0:n], ACT.Silu), "act", "gate_read")
                    else:
                        cw = conv[:, bass.ds(j, 1), :] if not isinstance(j, int) else conv[:, j:j + 1, :]
                        ct = inc(AC.activation(SG[:, 0:n], PS[0][:, 0:n], ACT.Copy, scale=cw[:, 0, 1:2]), "act")
                        wait(VE, ct)
                        for a, b, _ in segs:
                            v1 = inc(VE.scalar_tensor_tensor(SG[:, a + 1:b], PS[0][:, a:b - 1], cw[:, 0, 0:1],
                                                             SG[:, a + 1:b], ALU.mult, ALU.add), "dve")
                        wait(VE, v1)
                        for a, b, _ in segs:
                            v2 = inc(VE.scalar_tensor_tensor(SG[:, a:b - 1], PS[0][:, a + 1:b], cw[:, 0, 2:3],
                                                             SG[:, a:b - 1], ALU.mult, ALU.add), "dve", "gate_read")
                        wait(AC, v2)
                        sg = inc(AC.activation(SG[:, 0:n], SG[:, 0:n], ACT.Silu), "act")
                    if nx[0] is not None:
                        refill(0, nx[0])
                    wait(VE, u, sg, hf_free)
                    hf = inc(VE.tensor_tensor(HF[:, 0:n], SG[:, 0:n], PS[1][:, 0:n], ALU.mult), "dve", "up_read")
                    wait(AC, hf)
                    at = jj if isinstance(jj, int) else jj
                    dh = DH[:, at, 0:n] if isinstance(at, int) else DH[:, bass.ds(at, 1), 0:n].rearrange("p a t -> p (a t)")
                    dl = DL[:, at, 0:n] if isinstance(at, int) else DL[:, bass.ds(at, 1), 0:n].rearrange("p a t -> p (a t)")
                    hh = inc(AC.activation(dh, HF[:, 0:n], ACT.Copy), "act")
                    wait(VE, hh)
                    inc(VE.tensor_tensor(dl, HF[:, 0:n], dh.bitcast(F32), ALU.subtract), "dve", "hf_free")
                    if nx[1] is not None:
                        refill(1, nx[1])
                    if ada is not None and part is not None and not (isinstance(part, int) and part == NA - 1):
                        ada_next(ada, part, buf)

                def down(ch, m, half, free, nx):
                    o = product(half, PS[half], (DH, DL), FC, segs, (free,))
                    if nx is not None:
                        refill(half, nx)
                    wait(VE, o)
                    for a, b, j in segs:
                        gv = MOD[:, l, 24 + 16 + m, j:j + 1] if isinstance(m, int) else \
                            MOD[:, l, bass.ds(m + 40, 1), j]
                        xx = X[:, m, a:b] if isinstance(m, int) else X[:, bass.ds(m, 1), a:b].rearrange("p k t -> p (k t)")
                        v = inc(VE.scalar_tensor_tensor(xx, PS[half][:, a:b], gv, xx, ALU.mult, ALU.add),
                                "dve", f"down_read{half}")
                    if ch == CH - 1:
                        squares_add(m, half, n, wk, v)

                for ch in range(CH):
                    with c.fori(f"up{tag}{ch}", FC - 1) as i:
                        j = i + ch * FC
                        hidden(j, i, c.prev("gate_read"), c.prev("up_read"), c.prev("up_read"), c.prev("hf_free"),
                               (win_unit(j + 1, 0), win_unit(j + 1, 1)), ready if ch == 0 else (),
                               i if ch == 0 else None)
                    hidden(ch * FC + FC - 1, FC - 1, c.last["gate_read"], c.last["up_read"], c.last["up_read"],
                           c.last["hf_free"], (down_unit(ch, 0), down_unit(ch, 1)), part=FC - 1 + ch)
                    wait(PE, c.now("dve"))
                    if ch == CH - 1:
                        wait(AC, c.now("dve"))
                        squares_start(n, wk)
                    with c.fori(f"down{tag}{ch}", KT // 2 - 1) as i:
                        for half in range(2):
                            down(ch, i * 2 + half, half, c.prev(f"down_read{half}"), down_unit(ch, i * 2 + (half + 2)))
                    for half in range(2):
                        after = win_unit(FC, half) if ch == 0 else nxt[half]
                        down(ch, KT - 2 + half, half, c.last[f"down_read{half}"], after)
                    if ch == 0:
                        wait(PE, c.now("dve"))
                if ada is not None:
                    ada_finish(ada)

        def attention(ready):
            wq = dram["wqkv"]

            def unit(n):
                return wq[n], UNIT

            with ExitStack() as st:
                Q = sb("aQ", [P, 8, T], F32, st)
                KC = L + S + 2 * P
                K2 = sb("aK", [P, 4, 2, KC], F32R, st)
                MKB = sb("aMKB", [P, 4, 3 * P], BF16, st)
                V = sb("aV", [P, 8, L], F32, st)
                with ExitStack() as s2:
                    RAW = [sb(f"aR{i}", [P, T], F32, s2) for i in range(2)]
                    SQ = sb("aSQ", [P, T], F32, s2)
                    RI = sb("aRI", [P, T], F32, s2)
                    T1 = SQ[:, 0:S]
                    T2 = sb("aT2", [P, S], F32, s2)
                    KF = sb("aKF", [P, T], F32, s2)
                    COS = sb("aCOS", [P, S], F32, s2)
                    SIN = sb("aSIN", [P, S], F32, s2)
                    BD = sb("aBD", [P, P], F32, s2)
                    QG = sb("aQG", [P, 2], F32, s2)
                    AR = sb("aAR", [P, 4, 512], F32, s2)
                    buf = (V[:, :, :].rearrange("p (a b) n -> p a (b n)", b=2), AR[:, :, :], KF[:, 0:512])
                    c.barrier(AC, VE, PO)
                    c.barrier(SP)
                    for t, name in ((COS, "cos64"), (SIN, "sin64"), (BD, "bd64"), (QG, "qkgain")):
                        tab = inc(SP.dma_start(t[:, :], dram[name]), "small", by=16)
                    mk = Q[:, 6:8, :].rearrange("p a b -> p (a b)")
                    tab = inc(SP.dma_start(mk, dram["mask"]), "small", by=16)
                    wait(VE, tab)
                    mkb = inc(VE.tensor_copy(MKB[:, :, :].rearrange("p b n -> p (b n)"), mk), "dve")
                    wait(AC, mkb)
                    wait(VE, tab)
                    wait(PO, tab)

                    def head_norm(half, ready, dst_x, dst_c, gain):
                        wait(AC, ready, c.before("rope"))
                        ra = inc(AC.activation(RAW[half][:, :], PS[half][:, 0:T], ACT.Copy), "act")
                        sq = inc(AC.activation(SQ[:, :], PS[half][:, 0:T], ACT.Square), "act", f"q_read{half}")
                        wait(PE, sq, mkb)
                        for a, b, _ in ALL:
                            m = PE.matmul(PS[2][:, a:b], BD[:, :], SQ[:, a:b], start=True, stop=True)
                        r = rsqrt(RI[:, :], PS[2][:, 0:T], SQ[:, :], inc(m, "pe"), "rs_read")
                        wait(VE, r, ra)
                        n1 = inc(VE.scalar_tensor_tensor(RAW[half][:, :], RAW[half][:, :], gain, RI[:, :],
                                                         ALU.mult, ALU.mult), "dve")
                        wait(PO, n1)
                        t1 = inc(PO.tensor_tensor(T1, RAW[half][:, 0:S], COS[:, :], ALU.mult), "pool")
                        wait(VE, n1)
                        VE.sem_inc(c.sem("held"), 1)
                        sw = inc(VE.stream_shuffle(T2[:, :], RAW[half][:, 0:S], list(range(16, 32)) + list(range(16))), "dve")
                        wait(AC, n1)
                        inc(AC.activation(dst_c, RAW[half][:, S:T], ACT.Copy), "act", "rope_c")
                        wait(VE, sw)
                        t2 = inc(VE.tensor_tensor(T2[:, :], T2[:, :], SIN[:, :], ALU.mult), "dve")
                        wait(VE, t2, t1)
                        return inc(VE.tensor_tensor(dst_x, T1, T2[:, :], ALU.add), "dve", "rope")

                    kfree = ()

                    def qk_tile(n, half, free, dst_x, dst_c, gain, nx, ready=(), part=None):
                        if part is not None:
                            for i in range(2):
                                ada_load(0, part, i, buf, c.before(f"adamm{i}"))
                        o = product(half, PS[half], (HH, HL), KT, ALL, (free,), ready)
                        refill(half, nx)
                        if part is not None:
                            ada_sum(0, part, buf)
                        wait(AC, *kfree)
                        wait(VE, *kfree)
                        head_norm(half, o, dst_x, dst_c, gain)

                    with c.fori("aq", 4) as i:
                        for half in range(2):
                            n = i * 2 + half
                            qk_tile(n, half, c.prev(f"q_read{half}"), at(Q, n, 0, S), at(Q, n, S, T), QG[:, 0:1],
                                    unit(i * 2 + (half + 2)), ready if half == 0 else (), i * 2 + (A0 + half))
                            ada_turn(i * 2 + (A0 + half), buf)
                    ada_finish(0, 4 * A0, NV)
                    wait(VE, c.now("pe"))
                    for t in (K2[:, :, :, L:L + P].bitcast(F32), K2[:, :, :, L + P + S:].bitcast(F32), V[:, 2, :], V[:, 7, :]):
                        inc(VE.memset(t, 0.0), "dve")
                    for half in range(2):
                        qk_tile(8 + half, half, c.last[f"q_read{half}"], KF[:, L:T], KF[:, 0:L], QG[:, 1:2], unit(10 + half))
                        for g in range(2):
                            own, other = slice(64 * g, 64 * g + 64), slice(64 - 64 * g, 128 - 64 * g)
                            kg = K2[:, 2 * half + g, :, :]
                            rope = c.last["rope"]
                            for a, b, z in ((0, L, 0), (L, T, P)):
                                src = KF[own, a:b]
                                wait(AC, rope, c.last["rope_c"])
                                h = inc(AC.activation(kg[own, 0, a + z:b + z], src, ACT.Copy), "act")
                                hi = kg[own, 0, a + z:b + z].bitcast(F32)
                                wait(VE, h)
                                inc(VE.tensor_tensor(kg[own, 1, a + z:b + z], src, hi, ALU.subtract), "dve")
                                inc(VE.tensor_tensor(kg[other, 0, a + z:b + z], src, hi, ALU.subtract), "dve", "kf_read")
                                inc(AC.activation(kg[other, 1, a + z:b + z], src, ACT.Copy), "act", "kf_read2")
                        if half == 0:
                            kfree = (c.last["kf_read"], c.last["kf_read2"])
                    wait(PE, c.now("act"), c.now("dve"))
                    for half in range(2):
                        o = product_rows(half, 4, 4 * half, L, range(6), lambda m: PS[m // 2][:, 512 * (m % 2):512 * (m % 2) + L],
                                         half == 0, half == 1)
                        refill(half, (dram["wo0"][half], UNIT))
                    wait(AC, o)
                    for m in range(6):
                        inc(AC.activation(V[:, m + 3 if m < 4 else m - 4, :], PS[m // 2][:, 512 * (m % 2):512 * (m % 2) + L],
                                          ACT.Copy), "act")
                    c.barrier()
                with ExitStack() as s2:
                    NB = 5 * P + 1
                    QS = sb("aQS", [P, 16, P], F32R, s2)
                    VS = sb("aVS", [P, 3, L], F32, s2)
                    PR = [sb(f"aP{i}", [P, NB], F32, s2) for i in range(3)]
                    PT = [sb(f"aPT{i}", [P, 10, P], F32, s2) for i in range(2)]
                    ID = sb("aID", [P, P], F32, s2)
                    IDB = sb("aIDB", [P, P], BF16, s2)
                    SK = sb("aSK", [1, 16], F32, s2)
                    NM = sb("aNM", [P, 16], F32, s2)
                    RSM = sb("aRSM", [P, 16], F32, s2)
                    c.barrier(SP)
                    inc(SP.dma_start(ID[:, :], dram["ident"]), "small", by=16)
                    tab = inc(SP.dma_start(SK[:, :], dram["sink"]), "small", by=16)
                    wait(VE, tab)
                    wait(PE, tab)
                    wait(AC, tab)
                    inc(VE.tensor_copy(IDB[:, :], ID[:, :]), "dve")
                    inc(VE.tensor_scalar(SK[:, :], SK[:, :], 8.0 * D, None, ALU.mult), "dve")
                    c.barrier()

                    def stack_q(cols):
                        for g in range(2):
                            own, other = slice(64 * g, 64 * g + 64), slice(64 - 64 * g, 128 - 64 * g)
                            dst = QS[:].rearrange("p (t g) n -> p g t n", g=2)
                            h = inc(AC.activation(dst[own, g], cols(own), ACT.Copy), "act")
                            wait(VE, h)
                            r = inc(VE.tensor_tensor(dst[other, g], cols(own), dst[own, g].bitcast(F32), ALU.subtract), "dve")
                        wait(PE, r)

                    def heads(nk, band, vtile, mask, out_cols):
                        w = nk * P
                        tok = {}

                        def scores(n):
                            p, g = n // 8, n % 2
                            kh, ps = K2[:, 2 * p + g, :, :], PS[n % 2]
                            wait(PE, tok.get(("exp", n - 2)))
                            PE.matmul(ps[:, w:w + 1], ONE[0:1, :], SK[:, n:n + 1], start=True, stop=True)
                            if mask is not None:
                                for a, b, o in ((L, 512, 0), (512, w, 512 - L)):
                                    PE.matmul(ps[:, a:b], IDB[:, :], mask(o, o + b - a), start=True, stop=False)
                                for f in range(2):
                                    for a, b, o in ((L, 512, 0), (512, w, 512 - L)):
                                        PE.matmul(ps[:, a:b], QS[:, n, :], band(kh[:, f, :], o, b - a), start=False, stop=f == 1)
                            for f in range(2):
                                m = PE.matmul(ps[:, 0:L], QS[:, n, :], kh[:, f, 0:L], start=f == 0, stop=f == 1)
                            tok["s", n] = inc(m, "pe")

                        def softmax1(n):
                            ps = PS[n % 2]
                            wait(VE, tok["s", n])
                            v = inc(VE.reduce_max(NM[:, n:n + 1], ps[:, 0:w + 1], AX), "dve")
                            wait(VE, v)
                            v = inc(VE.tensor_scalar(NM[:, n:n + 1], NM[:, n:n + 1], -0.125, None, ALU.mult), "dve")
                            wait(AC, v, tok.get(("t", n - 3)))
                            tok["exp", n] = inc(AC.activation(PR[n % 3][:, 0:w + 1], ps[:, 0:w + 1], ACT.Exp,
                                                              bias=NM[:, n:n + 1], scale=0.125,
                                                              accum_out=RSM[:, n:n + 1]), "act")

                        def softmax2(n):
                            wait(VE, tok["exp", n])
                            v = inc(VE.reciprocal(RSM[:, n:n + 1], RSM[:, n:n + 1]), "dve")
                            wait(VE, v)
                            tok["p", n] = inc(VE.tensor_scalar(PR[n % 3][:, 0:w], PR[n % 3][:, 0:w], RSM[:, n:n + 1], None,
                                                               ALU.mult), "dve")

                        def turn(n):
                            i0, pt = (n % 2) * nk, PT[(n // 2) % 2]
                            wait(PE, tok["p", n], tok.get(("e", n - 1)), tok.get(("ev", n - 1)))
                            for k in range(nk):
                                i = i0 + k
                                m = PE.transpose((PS[2] if i < 8 else PS[3])[:, (i % 8) * P:(i % 8 + 1) * P],
                                                 PR[n % 3][:, k * P:(k + 1) * P], ID[:, :])
                            tok["t", n] = inc(m, "pe")
                            wait(AC, tok["t", n], tok.get(("pv", n - n % 2 - 4)))
                            i1 = min(i0 + nk, 8)
                            tok["e", n] = inc(AC.activation(pt[:, i0:i1, :], PS[2][:, i0 * P:i1 * P].rearrange(
                                "p (a b) -> p a b", b=P), ACT.Copy), "act")
                            if i0 + nk > 8:
                                wait(VE, tok["t", n], tok.get(("pv", n - n % 2 - 4)))
                                tok["ev", n] = inc(VE.tensor_copy(pt[:, 8:10, :], PS[3][:, 0:2 * P].rearrange(
                                    "p (a b) -> p a b", b=P)), "dve")

                        def values(n):
                            t, pt = n // 2, PT[(n // 2) % 2]
                            p, j = t // 4, t % 4
                            wait(PE, tok["e", n], tok["e", n + 1], tok.get(("ev", n + 1)), tok.get("o_read") if j == 0 else None)
                            for k in range(nk):
                                for g in range(2):
                                    v0 = (2 * p + g) * 64
                                    m = PE.matmul(PS[3][64 * g:64 * g + 64, 512 + j * P:512 + (j + 1) * P],
                                                  vtile(k)[:, v0:v0 + 64], pt[:, g * nk + k, :],
                                                  start=(k == 0), stop=(k == nk - 1))
                            tok["pv", n] = inc(m, "pe")
                            if j == 3:
                                tok["o_read"] = split(out_cols(HH, p), out_cols(HL, p), PS[3][:, 512:1024].rearrange(
                                    "p (a b) -> p a b", b=P), tok["pv", n])

                        for step in range(16 + 4):
                            if step < 16:
                                scores(step)
                                softmax1(step)
                            if 0 <= step - 1 < 16:
                                softmax2(step - 1)
                            if 0 <= step - 2 < 16:
                                turn(step - 2)
                            if step >= 4 and step % 2 == 0:
                                values(step - 4)

                    with c.fori("ablk", S // P) as b:
                        c.barrier()
                        inc(PO.tensor_copy(VS[:, :, :], V[:, bass.ds(b + 2, 3), :]), "pool")
                        wait(PE, c.now("pool"))
                        stack_q(lambda r: Q[r, :, bass.ds(b * P, P)])
                        heads(5, lambda k, o, n: k[:, bass.ds(b * P + (L + o), n)],
                              lambda k: V[:, k, :] if k < 2 else VS[:, k - 2, :],
                              lambda o, e: MKB[:, bass.ds(b, 1), o:e].rearrange("p b n -> p (b n)"),
                              lambda H, p: H[:, 4 * p:4 * p + 4, bass.ds(b * P, P)])
                    c.barrier()
                    for b in range(L // P):
                        q0 = S + b * P
                        c.barrier()
                        stack_q(lambda r: Q[r, :, q0:q0 + P])
                        heads(2, None, lambda k: V[:, k, :], None, lambda H, p: H[:, 4 * p:4 * p + 4, q0:q0 + P])
                    c.barrier()

        def retention():
            U0 = -(S + P)
            NU = L + S - U0
            w = dram["wret"]
            with ExitStack() as st:
                Q = sb("rQ", [P, 2, S], F32, st)
                K = sb("rK", [P, 2, T], F32, st)
                V = sb("rV", [P, 6, 512], F32, st)
                G = sb("rG", [P, 4, S], F32, st)
                O = sb("rO", [P, 4, S], F32, st)
                AT = sb("rAT", [P, 6, S], F32, st)
                YH = sb("rYH", [P, 4, S], F32R, st)
                YL = sb("rYL", [P, 4, S], F32R, st)
                DC = sb("rDC", [P, NU], F32, st)
                DS = O[:].rearrange("p a b -> p (a b)")[:, 0:NU]
                TMP = AT[:].rearrange("p a b -> p (a b)")[:, 0:NU]
                MC = sb("rMC", [P, S], F32, st)
                COS = sb("rCOS", [P, S], F32, st)
                SIN = sb("rSIN", [P, S], F32, st)
                T1, T2 = AT[:, 0, :], AT[:, 1, :]
                ON = sb("rON", [P, P], F32, st)
                GG = sb("rGG", [P, 16], F32, st)
                LG = sb("rLG", [P, 8], F32, st)
                LT = [sb(f"rLT{i}", [P, 8], F32, st) for i in range(4)]
                c.barrier()
                c.barrier(SP)
                inc(SP.dma_start(COS[:, :], dram["cos256"]), "small", by=16)
                inc(SP.dma_start(SIN[:, :], dram["sin256"]), "small", by=16)
                inc(SP.dma_start(GG[:, :], dram["gngain"]), "small", by=16)
                tab = inc(SP.dma_start(LG[:, :], dram["decay"]), "small", by=16)
                for e in (VE, AC, PE, PO):
                    wait(e, tab)
                on = inc(VE.memset(ON[:, :], 1.0 / 512), "dve")

                def step(ins):
                    r = inc(ins, "dve")
                    wait(VE, r)
                    return r

                z, s1, s2, acc = (t[:, :] for t in LT)
                step(VE.tensor_scalar(s1, LG[:, :], -1.0, None, ALU.mult))
                r = step(VE.tensor_tensor(s1, s1, LG[:, :], ALU.max))
                wait(AC, r)
                r = inc(AC.activation(z, s1, ACT.Exp, scale=-1.0), "act")
                wait(VE, r)
                step(VE.tensor_scalar(s1, z, 2.0, None, ALU.add))
                step(VE.reciprocal(s1, s1))
                step(VE.tensor_tensor(s1, s1, z, ALU.mult))
                step(VE.tensor_tensor(s2, s1, s1, ALU.mult))
                step(VE.tensor_scalar(acc, s2, 1.0 / 17, 1.0 / 15, ALU.mult, ALU.add))
                for n in (13, 11, 9, 7, 5, 3, 1):
                    step(VE.tensor_tensor(acc, acc, s2, ALU.mult))
                    step(VE.tensor_scalar(acc, acc, 1.0 / n, None, ALU.add))
                step(VE.tensor_tensor(acc, acc, s1, ALU.mult))
                step(VE.tensor_scalar(LG[:, :], LG[:, :], 0.0, None, ALU.min))
                step(VE.scalar_tensor_tensor(LG[:, :], acc, -2.0, LG[:, :], ALU.mult, ALU.add))

                with c.fori("ret", 4) as h:
                    c.barrier()
                    c.barrier(SP)

                    def nx(n):
                        return w[h * 16 + n], UNIT

                    ds = inc(SP.dma_start(DS, dram["dist"]), "small", by=16)
                    wait(VE, ds)
                    lf, lb = LG[:, bass.ds(h, 1)], LG[:, bass.ds(h + 4, 1)]
                    v = inc(VE.tensor_scalar(DC[:, :], DS, 0.0, None, ALU.max), "dve")
                    v2 = inc(VE.tensor_scalar(TMP, DS, -1.0, 0.0, ALU.mult, ALU.max), "dve")
                    wait(AC, v2)
                    e1 = inc(AC.activation(DC[:, :], DC[:, :], ACT.Exp, scale=lf), "act")
                    e2 = inc(AC.activation(TMP, TMP, ACT.Exp, scale=lb), "act")
                    wait(VE, e2)
                    v1 = inc(VE.scalar_tensor_tensor(DC[:, :], DS, 0.0, DC[:, :], ALU.is_ge, ALU.mult), "dve")
                    v2 = inc(VE.scalar_tensor_tensor(TMP, DS, 0.0, TMP, ALU.is_le, ALU.mult), "dve")
                    wait(VE, v2)
                    dc = inc(VE.tensor_tensor(DC[:, :], DC[:, :], TMP, ALU.add), "dve")

                    def rope(pa, pb, dst, ready):
                        wait(VE, ready, dc)
                        step(VE.tensor_tensor(T1, pa[:, 0:S], COS[:, :], ALU.mult))
                        step(VE.tensor_tensor(T2, pb[:, 0:S], SIN[:, :], ALU.mult))
                        step(VE.tensor_tensor(dst[:, 0, 0:S], T1, T2, ALU.subtract))
                        step(VE.tensor_tensor(T1, pa[:, 0:S], SIN[:, :], ALU.mult))
                        step(VE.tensor_tensor(T2, pb[:, 0:S], COS[:, :], ALU.mult))
                        return step(VE.tensor_tensor(dst[:, 1, 0:S], T1, T2, ALU.add))

                    product(0, PS[0], (HH, HL), KT, IMG)
                    refill(0, nx(2))
                    o = product(1, PS[1], (HH, HL), KT, IMG)
                    refill(1, nx(3))
                    rq = rope(PS[0], PS[1], Q, o)
                    product(0, PS[2], (HH, HL), KT, ALL)
                    refill(0, nx(4))
                    o = product(1, PS[3], (HH, HL), KT, ALL)
                    refill(1, nx(5))
                    rk = rope(PS[2], PS[3], K, o)
                    wait(AC, o)
                    for a in range(2):
                        kc = inc(AC.activation(K[:, a, S:T], PS[2 + a][:, S:T], ACT.Copy), "act")
                    vb = [PS[m // 2][:, 512 * (m % 2):512 * (m % 2) + 512] for m in range(6)]
                    for n in range(4):
                        o = product_rows(n % 2, 2, 2 * n, 512, range(6), lambda m: vb[m], n == 0, n == 3,
                                         (rq, rk, kc) if n == 0 else ())
                        refill(n % 2, nx(6 + n))
                    wait(AC, o)
                    for m in range(6):
                        vr = inc(AC.activation(V[:, m, :], vb[m], ACT.Copy), "act")
                    gr = [None, None]
                    for n in range(4):
                        dst = PS[3][:, 512 * (n % 2):512 * (n % 2) + 512]
                        o = product(n % 2, dst, (HH, HL), KT, IMG, (gr[n % 2], rk))
                        refill(n % 2, nx(10 + n))
                        wait(AC, o)
                        gr[n % 2] = inc(AC.activation(G[:, n, :], dst, ACT.Silu), "act")
                    wait(PE, vr, rq)
                    rd = [None] * 4
                    for m in range(6):
                        d = PS[(m % 4) // 2][:, 512 * (m % 2):512 * (m % 2) + 512]
                        wait(PE, rd[m % 4])
                        for a in range(2):
                            mm = PE.matmul(d, K[:, a, m * P:(m + 1) * P], Q[:, a, :], start=(a == 0), stop=(a == 1))
                        sc = inc(mm, "pe")
                        if m < 4:
                            mt = DC[:, -U0 - P * m:-U0 - P * m + S]
                        else:
                            jj = m - 4
                            f0, b0 = L - P * jj - U0, -S - P * jj - U0
                            wait(VE, dc, rd[0])
                            mc = inc(VE.tensor_tensor(MC[:, :], DC[:, f0:f0 + S], DC[:, b0:b0 + S], ALU.add), "dve")
                            wait(VE, mc)
                            mt = MC[:, :]
                        wait(VE, sc)
                        rd[m % 4] = inc(VE.scalar_tensor_tensor(AT[:, m, :], d, 256 ** -0.5, mt, ALU.mult, ALU.mult), "dve")
                        if m >= 4:
                            wait(VE, rd[m % 4])
                    wait(PE, rd[1], *gr)
                    for e in range(4):
                        d = PS[2 + e // 2][:, 512 * (e % 2):512 * (e % 2) + 512]
                        for m in range(6):
                            mm = PE.matmul(d, V[:, m, e * P:(e + 1) * P], AT[:, m, :], start=(m == 0), stop=(m == 5))
                        ov = inc(mm, "pe")
                        wait(AC, ov)
                        oc = inc(AC.activation(O[:, e, :], d, ACT.Copy), "act")
                    wait(PE, oc, rd[1])
                    for e in range(4):
                        mm = PE.matmul(PS[0][:, 0:S], ON[:, :], O[:, e, :], start=(e == 0), stop=(e == 3))
                    mu = inc(mm, "pe")
                    wait(VE, mu)
                    for e in range(4):
                        cen = inc(VE.tensor_tensor(O[:, e, :], O[:, e, :], PS[0][:, 0:S], ALU.subtract), "dve")
                        wait(AC, cen)
                        sq = inc(AC.activation(AT[:, e, :], O[:, e, :], ACT.Square), "act")
                        wait(PE, sq)
                        mm = PE.matmul(PS[0][:, S:2 * S], ON[:, :], AT[:, e, :], start=(e == 0), stop=(e == 3))
                    ri = rsqrt(AT[:, 4, :], PS[0][:, S:2 * S], AT[:, 5, :], inc(mm, "pe"))
                    wait(VE, ri)
                    for e in range(4):
                        gain = GG[:, bass.ds(h * 4 + e, 1)]
                        step(VE.scalar_tensor_tensor(O[:, e, :], O[:, e, :], gain, AT[:, 4, :], ALU.mult, ALU.mult))
                        y = step(VE.tensor_tensor(O[:, e, :], O[:, e, :], G[:, e, :], ALU.mult))
                        ys = split(YH[:, e, :], YL[:, e, :], O[:, e, :], y)
                    wait(PE, ys)
                    orr = [None, None]
                    for n in range(4):
                        half = n % 2
                        wait(PE, c.now(f"lo{half}"), orr[half])
                        for u in range(2):
                            i = 0
                            for k in range(4):
                                for wt, y in ((WH, YH), (WH, YL), (WL, YH)):
                                    col = (u * 4 + k) * P
                                    mm = PE.matmul(PS[half][:, 512 * u:512 * u + 512], wt[half][:, col:col + P], y[:, k, :],
                                                   start=(i == 0), stop=(i == 11))
                                    i += 1
                        o = inc(mm, f"mm{half}")
                        refill(half, nx(14 + n))
                        wait(VE, o)
                        for u in range(2):
                            orr[half] = inc(VE.scalar_tensor_tensor(X[:, 2 * n + u, 0:S], PS[half][:, 512 * u:512 * u + 512],
                                                                    MOD[:, 1, 16 + 2 * n + u, 0:1], X[:, 2 * n + u, 0:S],
                                                                    ALU.mult, ALU.add), "dve")
                c.barrier()

        def trunk_mixers(l, ready):
            segs = ALL if l == 2 else IMG
            n, nt = segs[-1][1], segs[-1][1] // P
            win = dram[f"zin{l}"]
            lam0 = 0.8 - 0.6 * float(np.exp(-0.3 * (l - 2)))

            def unit(u):
                return win[u], UNIT

            def flat(t, a, b):
                return t[:, a:b, :].rearrange("p a b -> p (a b)")

            with ExitStack() as st:
                Z = sb(f"Z{l}", [P, 12, T], F32, st)
                DK = sb(f"DK{l}", [P, 2, T], F32, st)
                AV = sb(f"AV{l}", [P, 6, L], F32, st)
                DV = sb(f"DV{l}", [P, 6, L], F32, st)
                BD = sb(f"BD{l}", [P, P], F32, st)
                SG = sb(f"SLG{l}", [P, 1], F32, st)
                LQ = sb(f"LQ{l}", [P, 4, 32], F32, st)
                LAM = sb(f"LAM{l}", [P, 4], F32, st)
                c.barrier(AC, VE, PO)
                c.barrier(SP)
                inc(SP.dma_start(BD[:, :], dram["bd64"]), "small", by=16)
                inc(SP.dma_start(SG[:, :], dram["subln"][l - 2]), "small", by=16)
                tab = inc(SP.dma_start(LQ[:, :, :], dram["lambda"][l - 2]), "small", by=16)

                def tile(i, half, free, dst, sg, nx, ready=()):
                    o = product(half, PS[half], (HH, HL), KT, sg, (free,), ready)
                    refill(half, nx)
                    wait(AC, o)
                    inc(AC.activation(dst, PS[half][:, 0:sg[-1][1]], ACT.Copy), "act", f"z_read{half}")

                with c.fori(f"z{l}", 6) as i:
                    for half in range(2):
                        tile(i, half, c.prev(f"z_read{half}"), at(Z, i * 2 + half, 0, n), segs, unit(i * 2 + (half + 2)),
                             ready if half == 0 else ())
                for half in range(2):
                    tile(12, half, c.last[f"z_read{half}"], DK[:, half, :], ALL, unit(14 + half), ready)
                wait(PE, c.now("act"))
                banks = [PS[m // 2][:, 512 * (m % 2):512 * (m % 2) + L] for m in range(6)]
                for u in range(2):
                    o = product_rows(u, 4, 4 * u, L, range(nt), lambda m: banks[m], u == 0, u == 1)
                    refill(u, unit(16 + u))
                wait(AC, o)
                for m in range(nt):
                    av = inc(AC.activation(AV[:, m, :], banks[m], ACT.Gelu_apprx_tanh), "act")
                wait(PE, av)
                for u in range(2):
                    o = product_rows(u, 4, 4 * u, L, range(6), lambda m: banks[m], u == 0, u == 1)
                    refill(u, (dram[f"zout{l}"][u], UNIT))
                wait(AC, o)
                for m in range(6):
                    inc(AC.activation(DV[:, m, :], banks[m], ACT.Copy), "act")
                c.barrier()

                with ExitStack() as s2:
                    T1 = sb(f"mT1{l}", [P, T], F32, s2)
                    T2 = sb(f"mT2{l}", [P, T], F32, s2)
                    with ExitStack() as s3:
                        WS = sb(f"WS{l}", [P, 4, P], F32, s3)
                        BS = sb(f"BS{l}", [P, 2, P], F32, s3)
                        COS = sb(f"mCOS{l}", [P, S], F32, s3)
                        SIN = sb(f"mSIN{l}", [P, S], F32, s3)
                        SW = sb(f"SW{l}", [P, 2, 3], F32, s3)
                        MS = [sb(f"MS{l}{i}", [P, 24], F32, s3) for i in range(3)]
                        inc(SP.dma_start(WS[:, :, :], dram["gmlp_w"][l - 2]), "small", by=16)
                        inc(SP.dma_start(BS[:, :, :], dram["gmlp_b"][l - 2]), "small", by=16)
                        inc(SP.dma_start(COS[:, :], dram["cos32"]), "small", by=16)
                        inc(SP.dma_start(SIN[:, :], dram["sin32"]), "small", by=16)
                        tab = inc(SP.dma_start(SW[:, :, :], dram["sconv"][l - 2]), "small", by=16)
                        for e in (PE, VE, AC, PO):
                            wait(e, tab)
                        u_ = inc(AC.activation(Z[:, 0:2, 0:n], Z[:, 0:2, 0:n], ACT.Gelu_apprx_tanh), "act")
                        g = 4 * nt
                        ms, m1, m2 = (t[:, 0:g] for t in MS)
                        for q in range(2):
                            mm = nt // 2
                            sq = inc(AC.activation(T1[:, 0:mm * L], flat(AV, q * mm, (q + 1) * mm), ACT.Square), "act")
                            wait(VE, sq)
                            v = inc(VE.reduce_sum(MS[0][:, q * 4 * mm:(q + 1) * 4 * mm],
                                                  T1[:, 0:mm * L].rearrange("p (a b) -> p a b", b=64), AX), "dve")
                            wait(AC, v)
                        wait(VE, v)
                        v = inc(VE.tensor_scalar(ms, ms, 1.0 / 64, None, ALU.mult), "dve")
                        r = rsqrt(m1, ms, m2, v)
                        wait(VE, r)
                        av4 = AV[:, 0:nt, :].rearrange("p m (h d) -> p (m h) d", d=64)
                        v = inc(VE.tensor_tensor(av4, av4, m1.unsqueeze(2).to_broadcast([P, g, 64]), ALU.mult), "dve")
                        wait(PE, v)
                        for h in range(4):
                            for m in range(nt):
                                mm = PE.matmul(PS[h // 2][64 * (h % 2):64 * (h % 2) + 64, m * P:(m + 1) * P],
                                               AV[:, m, 64 * h:64 * h + 64], WS[:, h, :], start=True, stop=True)
                        mx = inc(mm, "pe")
                        wait(VE, mx, u_)
                        for t in range(2):
                            v = inc(VE.tensor_tensor(T1[:, 0:n].rearrange("p (m q) -> p m q", q=P),
                                                     PS[t][:, 0:n].rearrange("p (m q) -> p m q", q=P),
                                                     BS[:, t:t + 1, :].to_broadcast([P, nt, P]), ALU.add), "dve")
                            wait(VE, v)
                            v = inc(VE.tensor_tensor(T1[:, 0:n], T1[:, 0:n], Z[:, t, 0:n], ALU.mult), "dve")
                            wait(VE, split(HH[:, t, 0:n], HL[:, t, 0:n], T1[:, 0:n], v))

                        for t in range(2):
                            v = inc(VE.tensor_tensor(T1[:, 0:n], Z[:, 6 + t, 0:n], Z[:, 2 + t, 0:n], ALU.mult), "dve")
                            wait(AC, v)
                            ct = inc(AC.activation(T2[:, 0:n], T1[:, 0:n], ACT.Copy, scale=SW[:, t, 1:2]), "act")
                            wait(VE, ct)
                            for a, b, _ in segs:
                                v = inc(VE.scalar_tensor_tensor(T2[:, a + 1:b], T1[:, a:b - 1], SW[:, t, 0:1],
                                                                T2[:, a + 1:b], ALU.mult, ALU.add), "dve")
                            wait(VE, v)
                            for a, b, _ in segs:
                                v = inc(VE.scalar_tensor_tensor(T2[:, a:b - 1], T1[:, a + 1:b], SW[:, t, 2:3],
                                                                T2[:, a:b - 1], ALU.mult, ALU.add), "dve")
                            wait(VE, v)
                            v = inc(VE.tensor_tensor(T2[:, 0:n], T2[:, 0:n], Z[:, 4 + t, 0:n], ALU.mult), "dve")
                            wait(VE, split(HH[:, 2 + t, 0:n], HL[:, 2 + t, 0:n], T2[:, 0:n], v))

                        for t in range(4):
                            q = Z[:, 10 + t, 0:S] if t < 2 else DK[:, t - 2, 0:S]
                            sw = inc(VE.stream_shuffle(T1[:, 0:S], q, [i ^ 8 for i in range(32)]), "dve")
                            v = inc(VE.tensor_tensor(T2[:, 0:S], q, COS[:, :], ALU.mult), "dve")
                            wait(VE, v)
                            v = inc(VE.tensor_tensor(T1[:, 0:S], T1[:, 0:S], SIN[:, :], ALU.mult), "dve")
                            wait(VE, v)
                            v = inc(VE.tensor_tensor(q, T1[:, 0:S], T2[:, 0:S], ALU.add), "dve")
                            wait(VE, v)
                            VE.sem_inc(c.sem("held"), 1)
                        c.barrier()

                    with ExitStack() as s3:
                        CS = sb(f"CS{l}", [P, 2 * P], F32, s3)
                        CN = sb(f"CN{l}", [P, 2, 4, S], F32, s3)
                        Y = flat(Z, 0, 4).rearrange("p (m t d) -> p m t d", m=6, t=2)
                        c.barrier(SP)
                        inc(SP.dma_start(CS[:, :], dram["dft64"]), "small", by=16)
                        tab = inc(SP.dma_start(CN[:, :, :, :], dram["dft512"]), "small", by=16)
                        wait(PE, tab)
                        for m in range(nt):
                            for t in range(2):
                                d = PS[m % 2][:, 512 * t:512 * t + 2 * P]
                                if m >= 2 and t == 0:
                                    wait(PE, yr[m % 2])
                                mm = PE.matmul(d, Z[:, 8 + t, m * P:(m + 1) * P], CS[:, :], start=True, stop=True)
                            o = inc(mm, "pe")
                            if m == 0:
                                yr = [None, None]
                            wait(AC, o)
                            yr[m % 2] = inc(AC.activation(Y[:, m, :, :], PS[m % 2][:, :].rearrange(
                                "p (t d) -> p t d", t=2)[:, :, 0:2 * P], ACT.Copy), "act")
                        wait(PE, *yr)

                        def tokens_dft(t, a, cn, m0, nm, w):
                            i = 0
                            for m in range(nm):
                                for q in range(2):
                                    mm = PE.matmul(PS[2 + t][:, a:a + w], Y[:, m0 + m, t, q * P:(q + 1) * P], cn(q, m),
                                                   start=(i == 0), stop=(i == 2 * nm - 1))
                                    i += 1
                            return inc(mm, "pe")

                        for t in range(2):
                            o = tokens_dft(t, 0, lambda q, m: CN[:, q, m, :], 0, 4, S)
                            split(HH[:, 4 + t, 0:S], HL[:, 4 + t, 0:S], PS[2 + t][:, 0:S], o)
                        if n > S:
                            wait(SP, o)
                            cc = CN[:, :, 0, :].rearrange("p q (m k) -> p q m k", m=2)
                            tab = inc(SP.dma_start(CN[:, :, 0, :], dram["dft256"]), "small", by=16)
                            wait(PE, tab)
                            for t in range(2):
                                o = tokens_dft(t, S, lambda q, m: cc[:, q, m, :], 4, 2, L)
                                split(HH[:, 4 + t, S:T], HL[:, 4 + t, S:T], PS[2 + t][:, S:T], o)
                        c.barrier()

                with ExitStack() as s2:
                    QS = sb(f"dQS{l}", [P, 2, 2 * P], F32, s2)
                    PR = [[sb(f"dP{l}{m}{i}", [P, T], F32, s2) for i in range(3 - m)] for m in range(2)]
                    PT = [sb(f"dPT{l}{i}", [P, 6, P], F32, s2) for i in range(2)]
                    OD = sb(f"dOD{l}", [P, 2, T], F32, s2)
                    ID = sb(f"dID{l}", [P, P], F32, s2)
                    NM = sb(f"dNM{l}", [P, 8, 2], F32, s2)
                    RL = sb(f"dRL{l}", [P, 8, 2], F32, s2)
                    c.barrier(SP)
                    tab = inc(SP.dma_start(ID[:, :], dram["ident"]), "small", by=16)
                    wait(PE, tab)
                    wait(VE, tab)
                    wait(AC, tab)
                    v = inc(VE.tensor_tensor(LQ[:, 0:2, :], LQ[:, 0:2, :], LQ[:, 2:4, :], ALU.mult), "dve")
                    wait(VE, v)
                    v = inc(VE.reduce_sum(LAM[:, 0:2], LQ[:, 0:2, :], AX), "dve")
                    wait(AC, v)
                    e = inc(AC.activation(LAM[:, 0:2], LAM[:, 0:2], ACT.Exp), "act")
                    wait(VE, e)
                    v = inc(VE.tensor_tensor(LAM[:, 2:3], LAM[:, 0:1], LAM[:, 1:2], ALU.subtract), "dve")
                    wait(VE, v)
                    v = inc(VE.tensor_scalar(LAM[:, 2:3], LAM[:, 2:3], lam0, -1.0, ALU.add, ALU.mult), "dve")
                    inc(VE.tensor_scalar(SG[:, :], SG[:, :], 1.0 - lam0, None, ALU.mult), "dve")

                    def blocks(qs, k0, m0, nm, dst):
                        w = nm * P
                        tok = {}

                        def scores(n):
                            q, h = n // 4, n % 4
                            for mp in range(2):
                                wait(PE, tok.get(("exp", n - 1, mp)))
                                r = slice(64 * (h % 2) + 32 * mp, 64 * (h % 2) + 32 * mp + 32)
                                for a in range(0, w, 512):
                                    b = min(w, a + 512)
                                    mm = PE.matmul(PS[mp][:, a:b], qs[r, h // 2, q * P:(q + 1) * P], DK[r, h // 2, k0 + a:k0 + b],
                                                   start=True, stop=True, tile_position=(r.start, 0))
                                tok["s", n, mp] = inc(mm, "pe")

                        def softmax(n):
                            for mp in range(2):
                                nmx = NM[:, n, mp:mp + 1]
                                wait(VE, tok["s", n, mp])
                                v = inc(VE.reduce_max(nmx, PS[mp][:, 0:w], AX), "dve")
                                wait(VE, v)
                                v = inc(VE.tensor_scalar(nmx, nmx, -(32 ** -0.5), None, ALU.mult), "dve")
                                wait(AC, v, tok.get(("t", n - 3)) if mp == 0 else tok.get(("p", n - 2)))
                                tok["exp", n, mp] = inc(AC.activation(PR[mp][n % (3 - mp)][:, 0:w], PS[mp][:, 0:w], ACT.Exp, bias=nmx,
                                                                      scale=32 ** -0.5, accum_out=RL[:, n, mp:mp + 1]), "act")

                        def combine(n):
                            p0, p1, r = PR[0][n % 3], PR[1][n % 2], RL[:, n, :]
                            wait(VE, tok["exp", n, 1])
                            v = inc(VE.reciprocal(r, r), "dve")
                            wait(VE, v)
                            v = inc(VE.tensor_tensor(r[:, 1:2], r[:, 1:2], LAM[:, 2:3], ALU.mult), "dve")
                            v0 = inc(VE.tensor_scalar(p0[:, 0:w], p0[:, 0:w], r[:, 0:1], None, ALU.mult), "dve")
                            wait(VE, v0)
                            tok["p", n] = inc(VE.scalar_tensor_tensor(p0[:, 0:w], p1[:, 0:w], r[:, 1:2], p0[:, 0:w],
                                                                      ALU.mult, ALU.add), "dve")

                        def turn(n):
                            wait(PE, tok["p", n], tok.get(("e", n - 1)))
                            for m in range(nm):
                                mm = PE.transpose(PS[2][:, m * P:(m + 1) * P], PR[0][n % 3][:, m * P:(m + 1) * P], ID[:, :])
                            tok["t", n] = inc(mm, "pe")
                            wait(AC, tok["t", n], tok.get(("av", n - 2)))
                            tok["e", n] = inc(AC.activation(PT[n % 2][:, 0:nm, :], PS[2][:, 0:w].rearrange(
                                "p (a b) -> p a b", b=P), ACT.Copy), "act")

                        def values(n):
                            q, h = n // 4, n % 4
                            wait(PE, tok["e", n])
                            for m in range(nm):
                                mm = PE.matmul(PS[3][64 * (h % 2):64 * (h % 2) + 64, 512 * q + (h // 2) * P:512 * q + (h // 2 + 1) * P],
                                               DV[:, m0 + m, 64 * h:64 * h + 64], PT[n % 2][:, m, :], start=(m == 0), stop=(m == nm - 1))
                            tok["av", n] = inc(mm, "pe")
                            if h == 3:
                                wait(AC, tok["av", n])
                                inc(AC.activation(dst(q), PS[3][:, 512 * q:512 * q + 2 * P].rearrange("p (t q) -> p t q", t=2),
                                                  ACT.Copy), "act")

                        for step in range(8 + 3):
                            if step < 8:
                                scores(step)
                                softmax(step)
                            if 0 <= step - 1 < 8:
                                combine(step - 1)
                            if 0 <= step - 2 < 8:
                                turn(step - 2)
                            if 0 <= step - 3 < 8:
                                values(step - 3)

                    with c.fori(f"diff{l}", S // P // 2) as b:
                        c.barrier()
                        v = inc(VE.tensor_copy(QS[:, :, :], Z[:, 10:12, bass.ds(b * 2 * P, 2 * P)]), "dve")
                        wait(PE, v)
                        blocks(QS, 0, 0, 6, lambda q: OD[:, :, bass.ds(b * 2 * P + q * P, P)])
                    c.barrier()
                    if n > S:
                        blocks(Z[:, 10:12, S:T], S, 4, 2, lambda q: OD[:, :, S + q * P:S + (q + 1) * P])
                    c.barrier()
                    N1, N2 = PR[0][0], PR[0][1]
                    for t in range(2):
                        sq = inc(AC.activation(N1[:, 0:n], OD[:, t, 0:n], ACT.Square), "act")
                        wait(PE, sq)
                        for a, b, _ in segs:
                            mm = PE.matmul(PS[t][:, a:b], BD[:, :], N1[:, a:b], start=True, stop=True)
                        r = rsqrt(N2[:, 0:n], PS[t][:, 0:n], N1[:, 0:n], inc(mm, "pe"))
                        wait(VE, r)
                        v = inc(VE.scalar_tensor_tensor(OD[:, t, 0:n], OD[:, t, 0:n], SG[:, 0:1], N2[:, 0:n],
                                                        ALU.mult, ALU.mult), "dve")
                        wait(AC, split(HH[:, 6 + t, 0:n], HL[:, 6 + t, 0:n], OD[:, t, 0:n], v))
                    c.barrier()

        def final_norm(wk):
            with ExitStack() as st:
                RS = sb("fRS", [P, S], F32, st)
                RI = sb("fRI", [P, S], F32, st)
                FG = sb("fFG", [P, KT], F32, st)
                c.barrier(SP, VE, AC)
                tab = inc(SP.dma_start(FG[:, :], dram["finalg"]), "small", by=16)
                r = rsqrt(RI[:, :], PS[2][:, 0:S], RS[:, :], mean_square(S, IMG, wk, True))
                wait(VE, r, tab)
                for k in range(KT):
                    v = inc(VE.scalar_tensor_tensor(X[:, k, 0:S], X[:, k, 0:S], FG[:, k:k + 1], RI[:, :], ALU.mult, ALU.mult), "dve")
                    wait(SP, v)
                    inc(SP.dma_start(out[k], X[:, k, 0:S]), "stored", by=16)
                wait(SP, c.now("stored"))

        def first(name, n=1):
            return tuple((dram[name][i * n], UNIT) for i in range(2))

        def first_refills(name):
            for slot, unit in enumerate(first(name)):
                refill(slot, unit)

        @contextmanager
        def work():
            with ExitStack() as st:
                yield [sb(f"WK{c.cnt['pe']}_{i}", [P, T], F32, st) for i in range(3)]

        A0 = 4
        with ExitStack() as st:
            buf = [sb(f"AR0{i}", [P, 4, 512], F32, st) for i in range(2)] + [sb("EV0", [P, 512], F32, st)]
            buf = (buf[0][:, :, :], buf[1][:, :, :], buf[2][:, :])
            ada_start(0, buf)
            inc(SP.dma_start(X[:, :, :], dram["xt"].rearrange("p (k t) -> p k t", k=KT)), "xin", by=16)
            with c.fori("ada0", A0 - 1) as i:
                ada_sum(0, i, buf)
                ada_next(0, i, buf)
                ada_turn(i, buf)
            ada_sum(0, A0 - 1, buf)
            ada_turn(A0 - 1, buf)
            ada_finish(0, 0, 4 * A0)
        first_refills("wqkv")
        with work() as wk:
            ready = norm("0a", 0, 0, ALL, wk, False)
        attention(ready)
        with work() as wk:
            project("0", 0, 16, lambda n: dram["wo0"][n], ALL, first("win0"), wk)
            c.barrier(SP)
            ready = norm("0b", 0, 1, ALL, wk, True)
            ffn("0", 0, ALL, first("wret"), wk, ready, ada=1)
            norm("1a", 1, 0, ALL, wk, True)
        retention()
        with work() as wk:
            c.barrier(SP)
            ready = norm("1b", 1, 1, IMG, wk, False)
            ffn("1", 1, IMG, first("zin2"), wk, ready, ada=2)
        c.barrier(SP)
        wait(SP, c.now("xin"))
        c2 = inc(SP.dma_start(X[:, :, S:T], dram["xc2"].rearrange("p (k t) -> p k t", k=KT)), "xin", by=16)
        for e in (VE, AC, PO):
            wait(e, c2)
        for l in (2, 3):
            segs = ALL if l == 2 else IMG
            if l == 2:
                with work() as wk:
                    ready = norm("2a", 2, 0, ALL, wk, False)
            trunk_mixers(l, ready)
            with work() as wk:
                project(f"{l}", l, 16, lambda u: dram[f"zout{l}"][u], segs, first(f"win{l}"), wk)
                c.barrier(SP)
                ready = norm(f"{l}b", l, 1, segs, wk, True)
                ffn(f"{l}", l, segs, first("zin3") if l == 2 else (None, None), wk, ready, CW[:, l - 2, :, :],
                    ada=3 if l == 2 else None)
                if l == 2:
                    ready = norm("3a", 3, 0, ALL, wk, True)
                else:
                    final_norm(wk)


def rotary(dim, feature):
    f = np.float32
    half = dim // 4
    n = np.arange(S)
    inv = (f(10000.0) ** (-np.arange(0, dim // 2, 2, dtype=f) / f(dim // 2))).astype(f)
    pos = np.where(feature[:, None] < dim // 2, (n // 64)[None], (n % 64)[None]).astype(f)
    ang = pos * inv[feature % half][:, None]
    sign = np.where(feature % (dim // 2) < half, -1.0, 1.0).astype(f)[:, None]
    return np.cos(ang).astype(f), (np.sin(ang) * sign).astype(f)


def layout(x):
    f = np.float32
    a = {k: np.asarray(v) for k, v in x.items()}

    def cols(v):
        v = v.reshape(*v.shape[:-1], -1, P)
        return np.swapaxes(v, -1, -2)

    d = {}
    xt = np.concatenate([a["x"][0], a["ctx"][0]], 0).T
    d["xt"] = xt.reshape(KT, P, T).transpose(1, 0, 2).reshape(P, KT * T)
    cin = np.stack([np.stack([a["c"][0], a["c_ctx"]], 0), np.stack([a["c_2"][0], a["c_ctx_2"]], 0)], 0)
    d["cin"] = cin.reshape(2, 2, KT, P).transpose(3, 0, 2, 1).reshape(P, -1)
    adb = np.concatenate([a["ada_b"], a["b_ada_2"]], 0)
    d["adb"] = adb.reshape(4, NV, P).transpose(2, 0, 1).reshape(P, -1)
    g = np.stack([np.concatenate([a["norm1_g"], a["norm1_g_2"]], 0), np.concatenate([a["norm2_g"], a["norm2_g_2"]], 0)], 1)
    d["gn"] = g.reshape(4, 2, KT, P).transpose(3, 0, 1, 2).reshape(P, -1)
    sel = np.zeros((P, 2), f)
    for q in range(4):
        for j in range(2):
            sel[32 * q + j, j] = 1
    d["sel"] = sel
    w = np.concatenate([a["ada_w"], a["w_ada_2"]], 0)
    d["ada"] = w.reshape(4, 2, 4, P, 12, 512).transpose(0, 4, 1, 3, 2, 5).reshape(96, P, 4, 512)

    def units(w, kt):
        n = w.shape[1] // P
        return w.reshape(kt, P, n, P).transpose(2, 1, 0, 3).reshape(n, P, kt * P)

    w = a["attn_w_qkv"][0]
    heads = [h for p in range(2) for j in range(4) for h in ((2 * p) * 4 + j, (2 * p + 1) * 4 + j)]
    order = np.concatenate([np.arange(h * 64, h * 64 + 64) for h in heads])
    wv = w[:, 1280:].reshape(2, 4, P, L).transpose(0, 2, 1, 3).reshape(2, P, UNIT)
    d["wqkv"] = np.concatenate([units(w[:, order], KT), units(w[:, 1024:1280], KT), wv], 0)
    d["wo0"] = units(a["attn_w_o"][0][order], KT)
    d["sink"] = a["attn_sink"][0][heads].reshape(1, 16)
    d["qkgain"] = np.stack([np.tile(a["attn_q_norm"][0], 2), np.tile(a["attn_k_norm"][0], 2)], 1)
    d["bd64"] = np.kron(np.eye(2, dtype=f), np.full((64, 64), 1 / 64, f))
    d["ident"] = np.eye(P, dtype=f)
    d["cos64"], d["sin64"] = rotary(64, np.arange(P) % 64)
    r, n = np.arange(P)[:, None], np.arange(3 * P)[None, :]
    mask = []
    for b in range(4):
        key = b * P - P + n
        mask.append(np.where((n >= r) & (n - r <= 2 * P) & (key >= 0) & (key < S), 0.0, -1e31))
    d["mask"] = np.stack(mask, 1).reshape(P, -1).astype(f)
    w, wo = a["ret_w_qkvg"][0], a["ret_w_o"][0]
    pair = np.concatenate([np.arange(64), np.arange(128, 192), np.arange(64, 128), np.arange(192, 256)])
    parts = []
    for h in range(4):
        parts.append(units(w[:, 256 * h + pair], KT))
        parts.append(units(w[:, D + 256 * h + pair], KT))
        parts.append(w[:, 2 * D + 512 * h:2 * D + 512 * (h + 1)].reshape(4, 2, P, 512).transpose(0, 2, 1, 3).reshape(4, P, UNIT))
        parts.append(units(w[:, 4 * D + 512 * h:4 * D + 512 * (h + 1)], KT))
        u = wo[512 * h:512 * (h + 1)].reshape(4, P, 4, 2, P).transpose(2, 1, 3, 0, 4)
        parts.append(u.reshape(4, P, UNIT))
    wi = units(a["ffn_w_in"][1], KT)
    d["wret"] = np.concatenate(parts + [wi[0:1], wi[FT:FT + 1]], 0)
    fi = np.arange(P)
    d["cos256"], s256 = rotary(256, np.where(fi < 64, fi, fi + 64))
    d["sin256"] = -s256
    d["gngain"] = a["ret_gn_g"][0].reshape(16, P).T
    d["decay"] = np.broadcast_to(a["ret_decay_logit"][0].reshape(8), (P, 8))
    d["dist"] = (np.arange(-(S + P), L + S)[None, :] - np.arange(P)[:, None]).astype(f)
    d["xc2"] = a["ctx_2"][0].T.reshape(KT, P, L).transpose(1, 0, 2).reshape(P, KT * L)
    rows = lambda w: w.reshape(2, 4, P, L).transpose(0, 2, 1, 3).reshape(2, P, UNIT)
    for l in (2, 3):
        w = a["w_in_2"][l - 2]
        g = lambda i: w[:, i * 256:(i + 1) * 256]
        feats = np.concatenate([g(i) for i in (0, 2, 3, 4, 5, 6, 7)], 1)
        d[f"zin{l}"] = np.concatenate([units(feats, KT), rows(g(1)), rows(g(8))], 0)
        d[f"zout{l}"] = units(a["w_out_2"][l - 2], KT)
    d["gmlp_w"] = a["gmlp_ws_2"].transpose(0, 3, 1, 2)
    d["gmlp_b"] = np.repeat(a["gmlp_bs_2"].reshape(2, 2, 2, P).transpose(0, 2, 1, 3), 64, axis=1)
    d["sconv"] = a["sconv_w_2"].reshape(2, 3, 2, P).transpose(0, 3, 2, 1)
    d["ffnconv"] = a["ffn_conv_w_2"].reshape(2, 3, FT, P).transpose(3, 0, 2, 1)
    lam = np.stack([a["lambda_q1_2"], a["lambda_q2_2"], a["lambda_k1_2"], a["lambda_k2_2"]], 1)
    d["lambda"] = np.broadcast_to(lam[:, None], (2, P, 4, 32))
    d["subln"] = np.tile(a["subln_g_2"], (1, 2)).reshape(2, P, 1)
    d["finalg"] = a["final_g_2"].reshape(KT, P).T
    d["cos32"], d["sin32"] = rotary(32, np.arange(P) % 32)

    def dft(n, fn):
        i = np.arange(n)
        return fn(2 * np.pi * (np.outer(i, i) % n) / n) / np.sqrt(n)

    d["dft64"] = np.concatenate([np.kron(np.eye(2), dft(64, np.cos)), np.kron(np.eye(2), dft(64, np.sin))], 1).astype(f)
    for n in (S, L):
        cs = np.stack([dft(n, np.cos), -dft(n, np.sin)], 0)
        cs = cs.reshape(2, n // P, P, n).transpose(2, 0, 1, 3)
        d[f"dft{n}"] = (cs if n == S else cs.reshape(P, 2, 2 * L)).astype(f)
    for l in range(4):
        wi = (a["ffn_w_in"] if l < 2 else a["ffn_w_up_2"])[l % 2]
        u = units(wi, KT)
        d[f"win{l}"] = np.stack([u[:FT], u[FT:]], 1).reshape(2 * FT, P, UNIT)
        wd = (a["ffn_w_out"] if l < 2 else a["ffn_w_down_2"])[l % 2]
        d[f"wdn{l}"] = np.concatenate([units(wd[c * FC * P:(c + 1) * FC * P], FC) for c in range(CH)], 0)
    return {k: np.ascontiguousarray(v, dtype=v.dtype) for k, v in d.items()}


def program(shapes, nc_of):
    book = {}
    for dry in (True, False):
        nc = nc_of()
        dram = {k: nc.dram_tensor(f"in_{k}", s, F32, kind="ExternalInput").ap() for k, s in shapes.items()}
        out = nc.dram_tensor("out_x", (KT, P, S), F32, kind="ExternalOutput").ap()
        build(nc, dram, out, book, dry)
    return nc


def kernel(**inputs):
    import concourse.bacc as _bacc
    from concourse.bass_utils import run_bass_kernel_spmd as _run

    arrays = layout(inputs)
    nc = program({k: v.shape for k, v in arrays.items()},
                 lambda: _bacc.Bacc("TRN2", target_bir_lowering=False, num_devices=1))
    r = _run(nc, [{f"in_{k}": v for k, v in arrays.items()}], core_ids=[0])
    got = r.results[0]["out_x"]
    return np.ascontiguousarray(got.reshape(D, S).T.reshape(1, S, D))
```

```python
from contextlib import ExitStack, contextmanager

import concourse.bass as bass
from concourse import mybir
import numpy as np

ALU = mybir.AluOpType
ACT = mybir.ActivationFunctionType
F32 = mybir.dt.float32
F32R = mybir.dt.float32r
BF16 = mybir.dt.bfloat16
AX = mybir.AxisListType.X

P = 128
D = 1024
KT = D // P
S = 512
L = 256
T = S + L
FF = 2816
FT = FF // P
CH = 2
FC = FT // CH
NV = 6 * D // P
EPS = 1e-6
START = 96
UNIT = KT * P
DUNIT = FC * P
ALL = ((0, S, 0), (S, T, 1))
IMG = ((0, S, 0),)


class Count:

    def __init__(self, sem, value, loop):
        self.sem, self.value, self.loop = sem, value, loop


class Chip:

    def __init__(self, nc, ctx, book, dry):
        self.nc, self.ctx, self.book, self.dry = nc, ctx, book, dry
        self.sems, self.cnt, self.loop, self.last, self.past = {}, {}, None, {}, {}

    def sem(self, name):
        if name not in self.sems:
            self.sems[name] = self.ctx.enter_context(self.nc.semaphore(name))
            self.cnt[name] = 0
        return self.sems[name]

    def inc(self, ins, sem, name=None, by=1):
        ins.then_inc(self.sem(sem), by)
        self.cnt[sem] += by
        c = Count(sem, self.cnt[sem], self.loop)
        if name:
            self.name(c, name)
        return c

    def name(self, c, name):
        self.last[name] = c
        if self.loop:
            self.book[self.loop["name"]]["at"][name] = (c.sem, c.value - self.loop["base"].get(c.sem, 0))

    def now(self, sem):
        self.sem(sem)
        return Count(sem, self.cnt[sem], self.loop)

    def prev(self, name):
        lp = self.loop
        sem, at = self.book[lp["name"]]["at"].get(name, ("dve", 1))
        self.sem(sem)
        return Count(sem, lp["base"].get(sem, 0) + at - self.stride(sem), lp)

    def before(self, name):
        c = self.last.get(name)
        if self.loop is None or c is not None and c.loop is self.loop:
            return c
        return self.prev(name)

    def stride(self, sem):
        return self.book[self.loop["name"]]["step"].get(sem, 1)

    def wait(self, eng, *counts):
        top = {}
        for c in counts:
            if c is None:
                continue
            inside, v = c.loop is not None and c.loop is self.loop, c.value
            step = self.book[c.loop["name"]]["step"].get(c.sem, 0 if not self.dry else 1) if c.loop else 0
            if c.loop and not inside:
                v += (c.loop["n"] - 1) * step
            key = (c.sem, inside)
            if key not in top or v > top[key][0]:
                top[key] = (v, step if inside else 0)
        for key, (v, step) in top.items():
            past = (str(eng.engine), key)
            if v <= 0 and not step or self.past.get(past, 0) >= v > 0:
                continue
            self.past[past] = v
            assert v >= 1 or self.dry, (self.loop["name"], key, v)
            eng.wait_ge(self.sem(key[0]), self.loop["i"] * step + v if step else v)

    @contextmanager
    def fori(self, name, n):
        rec = self.book.setdefault(name, {"step": {}, "at": {}})
        base = dict(self.cnt)
        with self.nc.Fori(0, n) as i:
            self.past = {}
            self.loop = {"name": name, "base": base, "i": i, "n": n}
            yield i
            steps = {s: v - base.get(s, 0) for s, v in self.cnt.items() if v != base.get(s, 0)}
            assert self.dry or rec["step"] == steps, (name, rec["step"], steps)
            rec["step"] = steps
            self.loop, self.past = None, {}
        for s, v in steps.items():
            self.cnt[s] = base.get(s, 0) + n * v

    def barrier(self, *engs):
        for e in engs or (self.nc.tensor, self.nc.scalar, self.nc.vector, self.nc.gpsimd):
            for s in ("pe", "act", "dve", "pool", "norm_act", "norm_dve"):
                if s in self.cnt and self.cnt[s]:
                    self.wait(e, self.now(s))


def build(nc, dram, out, book, dry):
    with ExitStack() as ctx:
        c = Chip(nc, ctx, book, dry)
        PE, AC, VE, PO, SP = nc.tensor, nc.scalar, nc.vector, nc.gpsimd, nc.sync
        wait, inc = c.wait, c.inc
        for eng, name in ((PE, "pe"), (AC, "act"), (VE, "dve"), (PO, "pool")):
            eng.sem_inc(c.sem(name), START)
            c.cnt[name] = START

        def sb(name, shape, dt=F32, stack=ctx):
            return stack.enter_context(nc.sbuf_tensor(name, shape, dt))

        X = sb("X", [P, KT, T])
        HH = sb("HH", [P, KT, T], F32R)
        HL = sb("HL", [P, KT, T], F32R)
        WR = [sb(f"WR{s}", [P, DUNIT]) for s in range(2)]
        WH = [sb(f"WH{s}", [P, DUNIT], F32R) for s in range(2)]
        WL = [sb(f"WL{s}", [P, DUNIT], F32R) for s in range(2)]
        MOD = sb("MOD", [P, 4, NV, 2])
        SCL = sb("SCL", [P, 4, 2, KT, 2])
        CAC = sb("CAC", [P, 2, KT, 32])
        CIN = sb("CIN", [P, 2, KT, 2])
        ADB = sb("ADB", [P, 4, NV])
        GN = sb("GN", [P, 4, 2, KT])
        SEL = sb("SEL", [P, 2])
        ONE = sb("ONE", [P, P])
        EPSC = sb("EPSC", [P, 1])
        NUL = sb("NUL", [P, 1])
        PS = [ctx.enter_context(nc.psum_tensor(f"PS{b}", [P, 1024], F32)) for b in range(4)]

        def lanes(pair, n):
            return PS[pair][:, 0:n]

        def refill_hi(slot, src, n):
            wait(SP, c.now(f"lo{slot}"))
            inc(SP.dma_start(WR[slot][:, 0:n], src), f"ld{slot}", by=16)
            wait(AC, c.now(f"ld{slot}"), c.now(f"mm{slot}"))
            inc(AC.activation(WH[slot][:, 0:n], WR[slot][:, 0:n], ACT.Copy), f"hi{slot}")

        def refill_lo(slot, n):
            wait(VE, c.now(f"hi{slot}"))
            inc(VE.tensor_tensor(WL[slot][:, 0:n], WR[slot][:, 0:n], WH[slot][:, 0:n].bitcast(F32), ALU.subtract),
                f"lo{slot}")

        def refill(slot, unit):
            if unit is not None:
                refill_hi(slot, *unit)
                refill_lo(slot, unit[1])

        def product(slot, dst, src, nk, segs, free=(), ready=()):
            wait(PE, c.now(f"lo{slot}"), *free)
            sh, sl = src
            n = 3 * nk
            i = 0
            for k in range(nk):
                wait(PE, *ready[k:k + 1])
                for w, h in ((WH, sh), (WH, sl), (WL, sh)):
                    for a, b, _ in segs:
                        m = PE.matmul(dst[:, a:b], w[slot][:, k * P:(k + 1) * P], h[:, k, a:b],
                                      start=(i == 0), stop=(i == n - 1))
                    i += 1
            return inc(m, f"mm{slot}")

        def rsqrt(dst, var, tmp, ready, name=None, dve="dve"):
            wait(AC, ready)
            y = inc(AC.activation(dst, var, ACT.Abs_reciprocal_sqrt, bias=EPSC[:, 0:1]), "act")
            wait(AC, y)
            h = inc(AC.activation(tmp, dst, ACT.Square, scale=0.5 ** 0.5), "act")
            wait(VE, h)
            u = inc(VE.scalar_tensor_tensor(tmp, var, EPS, tmp, ALU.add, ALU.mult), dve)
            wait(VE, u)
            return inc(VE.scalar_tensor_tensor(dst, tmp, 1.5, dst, ALU.subtract, ALU.mult, reverse0=True), dve, name)

        def at(t, i, a, b):
            return t[:, i, a:b] if isinstance(i, int) else t[:, bass.ds(i, 1), a:b].rearrange("p k t -> p (k t)")

        def split(hi, lo, src, ready, name=None, dve="dve"):
            wait(AC, ready)
            h = inc(AC.activation(hi, src, ACT.Copy), "act")
            wait(VE, h)
            return inc(VE.tensor_tensor(lo, src, hi.bitcast(F32), ALU.subtract), dve, name)

        def product_rows(slot, unit_k, k0, width, tiles, dst, first, last, free=(), ready=()):
            wait(PE, c.now(f"lo{slot}"), *free)
            for m in tiles:
                i = 0
                for k in range(unit_k):
                    wait(PE, *ready[k0 + k:k0 + k + 1])
                    for h, w in ((HH, WH), (HH, WL), (HL, WH)):
                        mm = PE.matmul(dst(m), h[:, k0 + k, m * P:(m + 1) * P], w[slot][:, k * width:(k + 1) * width],
                                       start=(first and i == 0), stop=(last and i == 3 * unit_k - 1))
                        i += 1
            return inc(mm, f"mm{slot}")

        def squares_start(n, wk):
            c.barrier(PO)
            inc(PO.memset(wk[2][:, 0:n], 0.0), "pool", "sq_add")

        def squares_add(k, half, n, wk, ready):
            wait(AC, ready, c.before(f"sq_add{half}") if c.loop else c.last.get(f"sq_add{half}"))
            sq = inc(AC.activation(wk[half][:, 0:n], at(X, k, 0, n), ACT.Square), "act", "sq")
            if not isinstance(k, int) or k < KT - 1:
                wait(PO, sq, c.before("sq_add"))
                a = inc(PO.tensor_tensor(wk[2][:, 0:n], wk[2][:, 0:n], wk[half][:, 0:n], ALU.add), "pool", "sq_add")
                c.name(a, f"sq_add{half}")

        def project(tag, l, gate, units, segs, nxt, wk, ready=()):
            c.barrier(AC, VE, PO)
            if not ready:
                c.barrier(PE)
            squares_start(segs[-1][1], wk)

            def tile(n, half, free, nx):
                o = product(half, PS[half], (HH, HL), KT, segs, (free,), ready if half == 0 and c.loop else ())
                refill(half, nx)
                wait(VE, o)
                for a, b, j in segs:
                    gv = MOD[:, l, gate + n, j:j + 1] if isinstance(n, int) else MOD[:, l, bass.ds(n + gate, 1), j]
                    xx = at(X, n, a, b)
                    v = inc(VE.scalar_tensor_tensor(xx, PS[half][:, a:b], gv, xx, ALU.mult, ALU.add),
                            "dve", f"out_read{half}")
                squares_add(n, half, segs[-1][1], wk, v)

            with c.fori(f"proj{tag}", KT // 2 - 1) as i:
                for half in range(2):
                    tile(i * 2 + half, half, c.prev(f"out_read{half}"), (units(i * 2 + (half + 2)), UNIT))
            for half in range(2):
                tile(KT - 2 + half, half, c.last[f"out_read{half}"], nxt[half])

        LG = sb("LG", [P, 8])
        loads = [(CIN, "cin"), (ADB, "adb"), (GN, "gn"), (SEL, "sel"), (LG, "decay")]
        CW = sb("CW", [P, 2, FT, 3])
        inc(SP.dma_start(CW[:, :, :, :], dram["ffnconv"]), "small", by=16)
        for t, name in loads:
            ap = t[:, :] if len(t.shape) == 2 else t[:].rearrange(
                {3: "p a b -> p (a b)", 4: "p a b c -> p (a b c)"}[len(t.shape)])
            inc(SP.dma_start(ap, dram[name]), "small", by=16)
        inc(VE.memset(ONE[:, :], 1.0 / D), "dve")
        inc(VE.memset(EPSC[:, :], EPS), "dve")
        z = inc(VE.memset(CAC[:, :, :, :], 0.0), "dve")
        wait(AC, z, c.now("small"))
        cact = inc(AC.activation(CAC[:, :, :, 0:2], CIN[:, :, :, :], ACT.Silu), "act")

        LT = [MOD[:, 3, 4 * i:4 * i + 4, :].rearrange("p a b -> p (a b)") for i in range(4)]
        wait(VE, c.now("small"))

        def step(ins):
            r = inc(ins, "dve")
            wait(VE, r)
            return r

        z, s1, s2, series = LT
        step(VE.tensor_scalar(s1, LG[:, :], -1.0, None, ALU.mult))
        r = step(VE.tensor_tensor(s1, s1, LG[:, :], ALU.max))
        wait(AC, r)
        r = inc(AC.activation(z, s1, ACT.Exp, scale=-1.0), "act")
        wait(VE, r)
        step(VE.tensor_scalar(s1, z, 2.0, None, ALU.add))
        step(VE.reciprocal(s1, s1))
        step(VE.tensor_tensor(s1, s1, z, ALU.mult))
        step(VE.tensor_tensor(s2, s1, s1, ALU.mult))
        step(VE.tensor_scalar(series, s2, 1.0 / 17, 1.0 / 15, ALU.mult, ALU.add))
        for n in (13, 11, 9, 7, 5, 3, 1):
            step(VE.tensor_tensor(series, series, s2, ALU.mult))
            step(VE.tensor_scalar(series, series, 1.0 / n, None, ALU.add))
        step(VE.tensor_tensor(series, series, s1, ALU.mult))
        step(VE.tensor_scalar(LG[:, :], LG[:, :], 0.0, None, ALU.min))
        step(VE.scalar_tensor_tensor(LG[:, :], series, -2.0, LG[:, :], ALU.mult, ALU.add))

        NA = 6 * D // 512
        acc, tr = PS[3][:, 0:512], PS[3][:, 512:512 + 2 * NV]

        def ada_load(l, nb, half, buf, free):
            wait(SP, free)
            inc(SP.dma_start(buf[half], dram["ada"][(nb + l * NA) * 2 + half]), f"ada{half}", by=16)

        def ada_start(l, buf):
            for half in range(2):
                ada_load(l, 0, half, buf, None)

        def ada_sum(l, nb, buf):
            wait(PE, cact)
            for half in range(2):
                wait(PE, c.now(f"ada{half}"), c.before("adaev") if half == 0 else None)
                for q in range(4):
                    m = PE.matmul(acc[32 * q:32 * q + 32, :], CAC[:, l // 2, 4 * half + q, :], buf[half][:, q, :],
                                  start=(half == 0), stop=(half == 1))
                done = inc(m, "pe", f"adamm{half}")
            wait(AC, done, c.before("adatr"))
            inc(AC.activation(buf[2], acc, ACT.Copy), "act", "adaev")

        def ada_next(l, nb, buf):
            for half in range(2):
                ada_load(l, nb + 1, half, buf, c.last[f"adamm{half}"])

        def ada_turn(nb, buf):
            wait(PE, c.last["adaev"])
            for s in range(4):
                dst = tr[:, bass.ds(nb * 8 + 2 * s, 2)] if not isinstance(nb, int) else tr[:, nb * 8 + 2 * s:nb * 8 + 2 * s + 2]
                m = PE.matmul(dst, buf[2][:, s * P:(s + 1) * P], SEL[:, :], start=True, stop=True)
            inc(m, "pe", "adatr")

        def ada_finish(l, v0=0, v1=NV):
            wait(VE, c.last["adatr"], c.now("small"))
            for j in range(2):
                v = inc(VE.tensor_tensor(MOD[:, l, v0:v1, j], tr.rearrange("p (v j) -> p v j", j=2)[:, v0:v1, j],
                                         ADB[:, l, v0:v1], ALU.add), "dve")
            wait(VE, v)
            for which in range(2):
                if v0 <= 24 * which + 8 and 24 * which + 16 <= v1:
                    for j in range(2):
                        inc(VE.scalar_tensor_tensor(SCL[:, l, which, :, j],
                                                    MOD[:, l, 24 * which + 8:24 * which + 16, j], 1.0,
                                                    GN[:, l, which, :], ALU.add, ALU.mult), "dve")

        def mean_square(n, segs, wk, summed):
            if summed:
                wait(PE, c.last["sq"], c.last["sq_add"])
                for i, t in enumerate((wk[2], wk[1])):
                    for a, b, _ in segs:
                        m = PE.matmul(PS[2][:, a:b], ONE[:, :], t[:, a:b], start=(i == 0), stop=(i == 1))
                return inc(m, "pe")
            pe = [None, None]
            for k in range(KT):
                wait(AC, pe[k % 2])
                sq = inc(AC.activation(wk[k % 2][:, 0:n], X[:, k, 0:n], ACT.Square), "act")
                wait(PE, sq)
                for a, b, _ in segs:
                    m = PE.matmul(PS[2][:, a:b], ONE[:, :], wk[k % 2][:, a:b], start=(k == 0), stop=(k == KT - 1))
                pe[k % 2] = inc(m, "pe")
            return pe[1]

        def norm(tag, l, which, segs, wk, summed):
            n = segs[-1][1]
            with ExitStack() as st:
                TT = [sb(f"TT{tag}{i}", [P, T], F32, st) for i in range(5)]
                RS = sb(f"RS{tag}", [P, T], F32, st)
                RI = sb(f"RI{tag}", [P, T], F32, st)
                c.barrier()
                if tag == "0a":
                    wait(AC, c.now("xin"))
                ri = rsqrt(RI[:, 0:n], PS[2][:, 0:n], RS[:, 0:n], mean_square(n, segs, wk, summed))
                wait(VE, ri)
                wait(PO, ri)
                pool = (3, 6)
                whole = {}
                for k in pool:
                    t = TT[3 + pool.index(k)]
                    p1 = inc(PO.tensor_tensor(t[:, 0:n], X[:, k, 0:n], RI[:, 0:n], ALU.mult), "pool")
                    wait(PO, p1)
                    for a, b, j in segs:
                        whole[k] = inc(PO.tensor_scalar(t[:, a:b], t[:, a:b], SCL[:, l, which, k, j:j + 1],
                                                        MOD[:, l, 24 * which + k, j:j + 1], ALU.mult, ALU.add), "pool")
                done, hi, slot = [None] * KT, [None] * KT, {}

                def rest(k):
                    wait(VE, hi[k])
                    if k in pool:
                        t = TT[3 + pool.index(k)]
                        done[k] = inc(VE.tensor_tensor(HL[:, k, 0:n], t[:, 0:n], HH[:, k, 0:n].bitcast(F32),
                                                       ALU.subtract), "norm_dve")
                        return
                    for a, b, j in segs:
                        done[k] = inc(VE.scalar_tensor_tensor(HL[:, k, a:b], slot[k][:, a:b], MOD[:, l, 24 * which + k, j:j + 1],
                                                              HH[:, k, a:b].bitcast(F32), ALU.add, ALU.subtract), "norm_dve")

                for k in range(KT):
                    if k in pool:
                        wait(AC, whole[k])
                        hi[k] = inc(AC.activation(HH[:, k, 0:n], TT[3 + pool.index(k)][:, 0:n], ACT.Copy), "norm_act")
                    else:
                        i = len(slot)
                        slot[k] = TT[i % 3]
                        wait(VE, done[k - 3] if i >= 3 else None, done[k - 4] if i >= 3 else None)
                        for a, b, j in segs:
                            v = inc(VE.scalar_tensor_tensor(slot[k][:, a:b], X[:, k, a:b], SCL[:, l, which, k, j:j + 1],
                                                            RI[:, a:b], ALU.mult, ALU.mult), "norm_dve")
                        wait(AC, v)
                        for a, b, j in segs:
                            hi[k] = inc(AC.activation(HH[:, k, a:b], slot[k][:, a:b], ACT.Identity,
                                                      bias=MOD[:, l, 24 * which + k, j:j + 1]), "norm_act")
                    if k:
                        rest(k - 1)
                rest(KT - 1)
                return done

        def ffn(tag, l, segs, nxt, wk, ready, conv=None, ada=None):
            n = segs[-1][1]
            win, wdn = dram[f"win{l}"], dram[f"wdn{l}"]

            def win_unit(j, half):
                return win[j * 2 + half], UNIT

            def down_unit(ch, m):
                return wdn[m + ch * KT], DUNIT

            with ExitStack() as st:
                DH = sb(f"DH{tag}", [P, FC, T], F32R, st)
                DL = sb(f"DL{tag}", [P, FC, T], F32R, st)
                SG, HF = wk[0:2]
                buf = [sb(f"AR{tag}_{i}", [P, 4, 512], F32, st) for i in range(2)] + [sb(f"EV{tag}_", [P, 512], F32, st)]
                buf = (buf[0][:, :, :], buf[1][:, :, :], buf[2][:, :])
                c.barrier(AC, VE, PO)
                if ada is not None:
                    ada_start(ada, buf)

                def hidden(j, jj, ev, free_up, sg_free, hf_free, nx, ready=(), part=None, after=()):
                    if c.loop:
                        inc(AC.activation(NUL[:, 0:1], EPSC[:, 0:1], ACT.Silu), "act")
                    g = product(0, PS[0], (HH, HL), KT, segs, (ev,) + after[:1], ready)
                    refill(0, nx[0])
                    if part is not None and ada is not None:
                        ada_sum(ada, part, buf)
                    u = product(1, PS[1], (HH, HL), KT, segs, (free_up,) + after[1:])
                    if part is not None and ada is not None:
                        ada_turn(part, buf)
                    wait(AC, g, sg_free)
                    if conv is None:
                        sg = inc(AC.activation(SG[:, 0:n], PS[0][:, 0:n], ACT.Silu), "act", "gate_read")
                    else:
                        cw = conv[:, bass.ds(j, 1), :] if not isinstance(j, int) else conv[:, j:j + 1, :]
                        ct = inc(AC.activation(SG[:, 0:n], PS[0][:, 0:n], ACT.Copy, scale=cw[:, 0, 1:2]), "act")
                        wait(VE, ct)
                        for a, b, _ in segs:
                            v1 = inc(VE.scalar_tensor_tensor(SG[:, a + 1:b], PS[0][:, a:b - 1], cw[:, 0, 0:1],
                                                             SG[:, a + 1:b], ALU.mult, ALU.add), "dve")
                        wait(VE, v1)
                        for a, b, _ in segs:
                            v2 = inc(VE.scalar_tensor_tensor(SG[:, a:b - 1], PS[0][:, a + 1:b], cw[:, 0, 2:3],
                                                             SG[:, a:b - 1], ALU.mult, ALU.add), "dve", "gate_read")
                        wait(AC, v2)
                        sg = inc(AC.activation(SG[:, 0:n], SG[:, 0:n], ACT.Silu), "act")
                    if c.loop:
                        refill(1, nx[1])
                    wait(VE, u, sg, hf_free)
                    hf = inc(VE.tensor_tensor(HF[:, 0:n], SG[:, 0:n], PS[1][:, 0:n], ALU.mult), "dve", "up_read")
                    wait(AC, hf)
                    dh, dl = at(DH, jj, 0, n), at(DL, jj, 0, n)
                    hh = inc(AC.activation(dh, HF[:, 0:n], ACT.Copy), "act")
                    wait(VE, hh)
                    inc(VE.tensor_tensor(dl, HF[:, 0:n], dh.bitcast(F32), ALU.subtract), "dve", "hf_free")
                    if not c.loop:
                        refill(1, nx[1])
                    if ada is not None and part is not None and not (isinstance(part, int) and part == NA - 1):
                        ada_next(ada, part, buf)

                def down(ch, m, half, free, nx, ready=()):
                    o = product(half, PS[half], (DH, DL), FC, segs, (free,), ready)
                    if nx is not None:
                        refill(half, nx)
                    wait(VE, o)
                    for a, b, j in segs:
                        gv = MOD[:, l, 24 + 16 + m, j:j + 1] if isinstance(m, int) else \
                            MOD[:, l, bass.ds(m + 40, 1), j]
                        xx = X[:, m, a:b] if isinstance(m, int) else X[:, bass.ds(m, 1), a:b].rearrange("p k t -> p (k t)")
                        v = inc(VE.scalar_tensor_tensor(xx, PS[half][:, a:b], gv, xx, ALU.mult, ALU.add),
                                "dve", f"down_read{half}")
                    if ch == CH - 1:
                        squares_add(m, half, n, wk, v)

                for ch in range(CH):
                    c0 = dict(c.last)
                    with c.fori(f"up{tag}{ch}", FC - 1) as i:
                        j = i + ch * FC
                        hidden(j, i, c.prev("gate_read"), c.prev("up_read"), c.prev("up_read"), c.prev("hf_free"),
                               (win_unit(j + 1, 0), win_unit(j + 1, 1)), ready if ch == 0 else (),
                               i if ch == 0 else None, (c0["down_read0"], c0["down_read1"]) if ch else ())
                    hidden(ch * FC + FC - 1, FC - 1, c.last["gate_read"], c.last["up_read"], c.last["up_read"],
                           c.last["hf_free"], (down_unit(ch, 0), down_unit(ch, 1)), part=FC - 1 + ch)
                    hidden_done = [None] * (FC - 1) + [c.last["hf_free"]]
                    wait(PE, c.last["gate_read"])
                    if ch == CH - 1:
                        wait(AC, c.now("dve"))
                        squares_start(n, wk)
                    with c.fori(f"down{tag}{ch}", KT // 2 - 1) as i:
                        for half in range(2):
                            down(ch, i * 2 + half, half, c.prev(f"down_read{half}"), down_unit(ch, i * 2 + (half + 2)),
                                 hidden_done if half == 0 else ())
                    for half in range(2):
                        after = win_unit(FC, half) if ch == 0 else nxt[half]
                        down(ch, KT - 2 + half, half, c.last[f"down_read{half}"], after)
                if ada is not None:
                    ada_finish(ada)

        def attention(ready):
            wq = dram["wqkv"]

            def unit(n):
                return wq[n], UNIT

            with ExitStack() as st:
                Q = sb("aQ", [P, 8, T], F32, st)
                KC = L + S + 2 * P
                K2 = sb("aK", [P, 4, 2, KC], F32R, st)
                MKB = sb("aMKB", [P, 4, 3 * P], BF16, st)
                V = sb("aV", [P, 8, L], F32, st)
                with ExitStack() as s2:
                    RAW = [sb(f"aR{i}", [P, T], F32, s2) for i in range(2)]
                    SQ = sb("aSQ", [P, T], F32, s2)
                    RI = sb("aRI", [P, T], F32, s2)
                    T1 = SQ[:, 0:S]
                    T2 = sb("aT2", [P, S], F32, s2)
                    KF = sb("aKF", [P, T], F32, s2)
                    COS = sb("aCOS", [P, S], F32, s2)
                    SIN = sb("aSIN", [P, S], F32, s2)
                    BD = sb("aBD", [P, P], F32, s2)
                    QG = sb("aQG", [P, 2], F32, s2)
                    AR = sb("aAR", [P, 4, 512], F32, s2)
                    buf = (V[:, :, :].rearrange("p (a b) n -> p a (b n)", b=2), AR[:, :, :], KF[:, 0:512])
                    c.barrier(AC, VE, PO)
                    for t, name in ((COS, "cos64"), (SIN, "sin64"), (BD, "bd64"), (QG, "qkgain")):
                        tab = inc(SP.dma_start(t[:, :], dram[name]), "small", by=16)
                    for i in range(2):
                        tab = inc(SP.dma_start(RAW[i][:, :], dram["mask"][:, i * T:(i + 1) * T]), "small", by=16)
                    wait(VE, tab)
                    for i in range(2):
                        mkb = inc(VE.tensor_copy(MKB[:, 2 * i:2 * i + 2, :].rearrange("p b n -> p (b n)"), RAW[i][:, :]), "dve")
                    wait(AC, mkb)
                    wait(VE, tab)
                    wait(PO, tab)

                    def head_norm(half, ready, dst_x, dst_c, gain, meanwhile):
                        wait(AC, ready, c.before("rope"))
                        ra = inc(AC.activation(RAW[half][:, :], PS[half][:, 0:T], ACT.Copy), "act")
                        sq = inc(AC.activation(SQ[:, :], PS[half][:, 0:T], ACT.Square), "act", f"q_read{half}")
                        meanwhile()
                        wait(PE, sq, mkb)
                        for a, b, _ in ALL:
                            m = PE.matmul(PS[2][:, a:b], BD[:, :], SQ[:, a:b], start=True, stop=True)
                        r = rsqrt(RI[:, :], PS[2][:, 0:T], SQ[:, :], inc(m, "pe"), "rs_read")
                        wait(VE, r, ra)
                        n1 = inc(VE.scalar_tensor_tensor(RAW[half][:, :], RAW[half][:, :], gain, RI[:, :],
                                                         ALU.mult, ALU.mult), "dve")
                        wait(PO, n1)
                        t1 = inc(PO.tensor_tensor(T1, RAW[half][:, 0:S], COS[:, :], ALU.mult), "pool")
                        wait(VE, n1)
                        VE.sem_inc(c.sem("held"), 1)
                        sw = inc(VE.stream_shuffle(T2[:, :], RAW[half][:, 0:S], list(range(16, 32)) + list(range(16))), "dve")
                        wait(AC, n1)
                        inc(AC.activation(dst_c, RAW[half][:, S:T], ACT.Copy), "act", "rope_c")
                        wait(VE, sw)
                        t2 = inc(VE.tensor_tensor(T2[:, :], T2[:, :], SIN[:, :], ALU.mult), "dve")
                        wait(VE, t2, t1)
                        return inc(VE.tensor_tensor(dst_x, T1, T2[:, :], ALU.add), "dve", "rope")

                    kfree = ()

                    def qk_tile(n, half, free, dst_x, dst_c, gain, nx, ready=(), part=None):
                        if part is not None:
                            for i in range(2):
                                ada_load(0, part, i, buf, c.before(f"adamm{i}"))
                        o = product(half, PS[half], (HH, HL), KT, ALL, (free,), ready)

                        def meanwhile():
                            refill(half, nx)
                            if part is not None:
                                ada_sum(0, part, buf)
                            wait(AC, *kfree)
                            wait(VE, *kfree)

                        head_norm(half, o, dst_x, dst_c, gain, meanwhile)

                    with c.fori("aq", 4) as i:
                        for half in range(2):
                            n = i * 2 + half
                            qk_tile(n, half, c.prev(f"q_read{half}"), at(Q, n, 0, S), at(Q, n, S, T), QG[:, 0:1],
                                    unit(i * 2 + (half + 2)), ready if half == 0 else (), i * 2 + (A0 + half))
                            ada_turn(i * 2 + (A0 + half), buf)
                    ada_finish(0, 4 * A0, NV)
                    wait(VE, c.now("pe"))
                    for t in (K2[:, :, :, L:L + P].bitcast(F32), K2[:, :, :, L + P + S:].bitcast(F32), V[:, 2, :], V[:, 7, :]):
                        inc(VE.memset(t, 0.0), "dve")
                    for half in range(2):
                        qk_tile(8 + half, half, c.last[f"q_read{half}"], KF[:, L:T], KF[:, 0:L], QG[:, 1:2], unit(10 + half))
                        for g in range(2):
                            own, other = slice(64 * g, 64 * g + 64), slice(64 - 64 * g, 128 - 64 * g)
                            kg = K2[:, 2 * half + g, :, :]
                            rope = c.last["rope"]
                            for a, b, z in ((0, L, 0), (L, T, P)):
                                src = KF[own, a:b]
                                wait(AC, rope, c.last["rope_c"])
                                h = inc(AC.activation(kg[own, 0, a + z:b + z], src, ACT.Copy), "act")
                                hi = kg[own, 0, a + z:b + z].bitcast(F32)
                                wait(VE, h)
                                inc(VE.tensor_tensor(kg[own, 1, a + z:b + z], src, hi, ALU.subtract), "dve")
                                inc(VE.tensor_tensor(kg[other, 0, a + z:b + z], src, hi, ALU.subtract), "dve", "kf_read")
                                inc(AC.activation(kg[other, 1, a + z:b + z], src, ACT.Copy), "act", "kf_read2")
                        if half == 0:
                            kfree = (c.last["kf_read"], c.last["kf_read2"])
                    wait(PE, c.last["q_read0"], c.last["q_read1"], c.last["rs_read"])
                    for half in range(2):
                        o = product_rows(half, 4, 4 * half, L, range(6), lambda m: PS[m // 2][:, 512 * (m % 2):512 * (m % 2) + L],
                                         half == 0, half == 1)
                        refill(half, (dram["wo0"][half], UNIT))
                    for m in range(6):
                        e, sem, copy = ((AC, "act", lambda d, x: AC.activation(d, x, ACT.Copy)), (VE, "dve", VE.tensor_copy))[m % 2]
                        wait(e, o)
                        inc(copy(V[:, m + 3 if m < 4 else m - 4, :], PS[m // 2][:, 512 * (m % 2):512 * (m % 2) + L]), sem)
                    c.barrier()
                with ExitStack() as s2:
                    NB = 5 * P + 1
                    QS = sb("aQS", [P, 16, P], F32R, s2)
                    VS = sb("aVS", [P, 3, L], F32, s2)
                    PR = [sb(f"aP{i}", [P, NB], F32, s2) for i in range(3)]
                    PT = [sb(f"aPT{i}", [P, 10, P], F32, s2) for i in range(2)]
                    ID = sb("aID", [P, P], F32, s2)
                    IDB = sb("aIDB", [P, P], BF16, s2)
                    SK = sb("aSK", [1, 16], F32, s2)
                    NM = sb("aNM", [P, 16], F32, s2)
                    RSM = sb("aRSM", [P, 16], F32, s2)
                    c.barrier(SP)
                    inc(SP.dma_start(ID[:, :], dram["ident"]), "small", by=16)
                    tab = inc(SP.dma_start(SK[:, :], dram["sink"]), "small", by=16)
                    wait(VE, tab)
                    wait(PE, tab)
                    wait(AC, tab)
                    inc(VE.tensor_copy(IDB[:, :], ID[:, :]), "dve")
                    inc(VE.tensor_scalar(SK[:, :], SK[:, :], 8.0 * D, None, ALU.mult), "dve")
                    c.barrier()

                    def stack_q(cols, free=None):
                        wait(AC, free)
                        wait(VE, free)
                        for g in range(2):
                            own, other = slice(64 * g, 64 * g + 64), slice(64 - 64 * g, 128 - 64 * g)
                            dst = QS[:].rearrange("p (t g) n -> p g t n", g=2)
                            h = inc(AC.activation(dst[own, g], cols(own), ACT.Copy), "act")
                            wait(VE, h)
                            r = inc(VE.tensor_tensor(dst[other, g], cols(own), dst[own, g].bitcast(F32), ALU.subtract), "dve")

                    def heads(nk, band, vtile, mask, out_cols, after, vs):
                        w = nk * P
                        tok = {}

                        def scores(n):
                            p, g = n // 8, n % 2
                            kh, ps = K2[:, 2 * p + g, :, :], PS[n % 2]
                            wait(PE, tok.get(("exp", n - 2)))
                            PE.matmul(ps[:, w:w + 1], ONE[0:1, :], SK[:, n:n + 1], start=True, stop=True)
                            if mask is not None:
                                for a, b, o in ((L, 512, 0), (512, w, 512 - L)):
                                    PE.matmul(ps[:, a:b], IDB[:, :], mask(o, o + b - a), start=True, stop=False)
                                for f in range(2):
                                    for a, b, o in ((L, 512, 0), (512, w, 512 - L)):
                                        PE.matmul(ps[:, a:b], QS[:, n, :], band(kh[:, f, :], o, b - a), start=False, stop=f == 1)
                            for f in range(2):
                                m = PE.matmul(ps[:, 0:L], QS[:, n, :], kh[:, f, 0:L], start=f == 0, stop=f == 1)
                            tok["s", n] = inc(m, "pe")

                        def softmax1(n):
                            ps = PS[n % 2]
                            wait(VE, tok["s", n])
                            v = inc(VE.reduce_max(NM[:, n:n + 1], ps[:, 0:w + 1], AX), "dve")
                            wait(VE, v)
                            v = inc(VE.tensor_scalar(NM[:, n:n + 1], NM[:, n:n + 1], -0.125, None, ALU.mult), "dve")
                            wait(AC, v, tok.get(("t", n - 3)))
                            tok["exp", n] = inc(AC.activation(PR[n % 3][:, 0:w + 1], ps[:, 0:w + 1], ACT.Exp,
                                                              bias=NM[:, n:n + 1], scale=0.125,
                                                              accum_out=RSM[:, n:n + 1]), "act")

                        def softmax2(n):
                            wait(VE, tok["exp", n])
                            v = inc(VE.reciprocal(RSM[:, n:n + 1], RSM[:, n:n + 1]), "dve")
                            wait(VE, v)
                            tok["p", n] = inc(VE.tensor_scalar(PR[n % 3][:, 0:w], PR[n % 3][:, 0:w], RSM[:, n:n + 1], None,
                                                               ALU.mult), "dve")

                        def turn(n):
                            g, pt, nb = n % 2, PT[(n // 2) % 2], min(nk, 4)
                            free = tok.get(("pv", n - g - 4))
                            wait(PE, tok["p", n], tok.get(("e", n - 2)))
                            for k in range(nk):
                                if k == 4:
                                    wait(PE, tok.get(("ev", n - 1)))
                                m = PE.transpose(PS[2][:, (4 * g + k) * P:(4 * g + k + 1) * P] if k < 4 else
                                                 PS[3][:, g * P:(g + 1) * P], PR[n % 3][:, k * P:(k + 1) * P], ID[:, :])
                            tok["t", n] = inc(m, "pe")
                            wait(AC, tok["t", n], free)
                            tok["e", n] = inc(AC.activation(pt[:, g * nk:g * nk + nb, :], PS[2][:, 4 * g * P:(4 * g + nb) * P].rearrange(
                                "p (a b) -> p a b", b=P), ACT.Copy), "act")
                            if nk > 4:
                                wait(VE, tok["t", n], free)
                                tok["ev", n] = inc(VE.tensor_copy(pt[:, g * nk + 4, :], PS[3][:, g * P:(g + 1) * P]), "dve")

                        def values(n):
                            t, pt = n // 2, PT[(n // 2) % 2]
                            p, j = t // 4, t % 4
                            wait(PE, vs, tok["e", n], tok["e", n + 1], tok.get(("ev", n + 1)), tok.get("o_read") if j == 0 else None)
                            for k in range(nk):
                                for g in range(2):
                                    v0 = (2 * p + g) * 64
                                    m = PE.matmul(PS[3][64 * g:64 * g + 64, 512 + j * P:512 + (j + 1) * P],
                                                  vtile(k)[:, v0:v0 + 64], pt[:, g * nk + k, :],
                                                  start=(k == 0), stop=(k == nk - 1))
                            tok["pv", n] = inc(m, "pe")
                            if j == 3:
                                tok["o_read"] = split(out_cols(HH, p), out_cols(HL, p), PS[3][:, 512:1024].rearrange(
                                    "p (a b) -> p a b", b=P), tok["pv", n])

                        for step in range(16 + 4):
                            if step < 16:
                                scores(step)
                                softmax1(step)
                            if step == 15 and after is not None:
                                stack_q(after, tok["s", 15])
                            if 0 <= step - 1 < 16:
                                softmax2(step - 1)
                            if 0 <= step - 2 < 16:
                                turn(step - 2)
                            if step >= 4 and step % 2 == 0:
                                values(step - 4)

                    def cols(q0):
                        return lambda r: Q[r, :, q0:q0 + P] if isinstance(q0, int) else Q[r, :, bass.ds(q0, P)]

                    stack_q(cols(0))
                    with c.fori("ablk", S // P) as b:
                        c.barrier()
                        vs = inc(PO.tensor_copy(VS[:, :, :], V[:, bass.ds(b + 2, 3), :]), "pool")
                        heads(5, lambda k, o, n: k[:, bass.ds(b * P + (L + o), n)],
                              lambda k: V[:, k, :] if k < 2 else VS[:, k - 2, :],
                              lambda o, e: MKB[:, bass.ds(b, 1), o:e].rearrange("p b n -> p (b n)"),
                              lambda H, p: H[:, 4 * p:4 * p + 4, bass.ds(b * P, P)], cols(b * P + P), vs)
                    for b in range(L // P):
                        q0 = S + b * P
                        c.barrier()
                        heads(2, None, lambda k: V[:, k, :], None, lambda H, p: H[:, 4 * p:4 * p + 4, q0:q0 + P],
                              cols(q0 + P) if b == 0 else None, None)
                    c.barrier()

        def retention(ready):
            U0 = -(S + P)
            NU = L + S - U0
            w = dram["wret"]
            with ExitStack() as st:
                Q = sb("rQ", [P, 2, S], F32, st)
                K = sb("rK", [P, 2, T], F32, st)
                V = sb("rV", [P, 6, 512], F32, st)
                G = sb("rG", [P, 4, S], F32, st)
                O = sb("rO", [P, 4, S], F32, st)
                AT = sb("rAT", [P, 6, S], F32, st)
                YH = sb("rYH", [P, 4, S], F32R, st)
                YL = sb("rYL", [P, 4, S], F32R, st)
                DC = sb("rDC", [P, NU], F32, st)
                DS = O[:].rearrange("p a b -> p (a b)")[:, 0:NU]
                TMP = AT[:].rearrange("p a b -> p (a b)")[:, 0:NU]
                MC = sb("rMC", [P, S], F32, st)
                COS = sb("rCOS", [P, S], F32, st)
                SIN = sb("rSIN", [P, S], F32, st)
                T1, T2 = AT[:, 0, :], AT[:, 1, :]
                ON = sb("rON", [P, P], F32, st)
                GG = sb("rGG", [P, 16], F32, st)
                c.barrier(AC, VE, PO, SP)
                inc(SP.dma_start(COS[:, :], dram["cos256"]), "small", by=16)
                inc(SP.dma_start(SIN[:, :], dram["sin256"]), "small", by=16)
                tab = inc(SP.dma_start(GG[:, :], dram["gngain"]), "small", by=16)
                for e in (VE, AC, PO, SP):
                    wait(e, tab)
                on = inc(VE.memset(ON[:, :], 1.0 / 512), "decay")

                with c.fori("ret", 4) as h:
                    c.barrier(AC, VE, PO, SP)
                    wait(PE, c.now("dve"), c.now("act"))

                    def nx(n):
                        return w[h * 16 + n], UNIT

                    ds = inc(SP.dma_start(DS, dram["dist"]), "small", by=16)

                    def rope(pa, pb, dst, ready):
                        wait(VE, ready)
                        step(VE.tensor_tensor(T1, pa[:, 0:S], COS[:, :], ALU.mult))
                        step(VE.tensor_tensor(T2, pb[:, 0:S], SIN[:, :], ALU.mult))
                        step(VE.tensor_tensor(dst[:, 0, 0:S], T1, T2, ALU.subtract))
                        step(VE.tensor_tensor(T1, pa[:, 0:S], SIN[:, :], ALU.mult))
                        step(VE.tensor_tensor(T2, pb[:, 0:S], COS[:, :], ALU.mult))
                        return step(VE.tensor_tensor(dst[:, 1, 0:S], T1, T2, ALU.add))

                    product(0, PS[0], (HH, HL), KT, IMG, (), ready)
                    refill(0, nx(2))
                    o = product(1, PS[1], (HH, HL), KT, IMG)
                    refill(1, nx(3))
                    rq = rope(PS[0], PS[1], Q, o)
                    product(0, PS[2], (HH, HL), KT, ALL)
                    refill(0, nx(4))
                    o = product(1, PS[3], (HH, HL), KT, ALL)
                    refill(1, nx(5))
                    rk = rope(PS[2], PS[3], K, o)
                    wait(AC, o)
                    for a in range(2):
                        kc = inc(AC.activation(K[:, a, S:T], PS[2 + a][:, S:T], ACT.Copy), "act")

                    def decay():
                        wait(VE, ds, rk)
                        lf, lb = LG[:, bass.ds(h, 1)], LG[:, bass.ds(h + 4, 1)]
                        v = inc(VE.tensor_scalar(DC[:, :], DS, 0.0, None, ALU.max), "dve")
                        v2 = inc(VE.tensor_scalar(TMP, DS, -1.0, 0.0, ALU.mult, ALU.max), "dve")
                        wait(AC, v2)
                        e1 = inc(AC.activation(DC[:, :], DC[:, :], ACT.Exp, scale=lf), "act")
                        e2 = inc(AC.activation(TMP, TMP, ACT.Exp, scale=lb), "act")
                        wait(VE, e2)
                        v1 = inc(VE.scalar_tensor_tensor(DC[:, :], DS, 0.0, DC[:, :], ALU.is_ge, ALU.mult), "dve")
                        v2 = inc(VE.scalar_tensor_tensor(TMP, DS, 0.0, TMP, ALU.is_le, ALU.mult), "dve")
                        wait(VE, v2)
                        dc = inc(VE.tensor_tensor(DC[:, :], DC[:, :], TMP, ALU.add), "dve")
                        return dc

                    gr = [None] * 4

                    def gate_read(e, dst, o, unit):
                        refill(e % 2, unit)
                        wait(AC, o)
                        gr[e] = inc(AC.activation(G[:, e, :], dst, ACT.Silu), "act")

                    for e in range(2):
                        gate_read(e, PS[e][:, 512:1024], product(e % 2, PS[e][:, 512:1024], (HH, HL), KT, IMG), nx(6 + e))
                    vb = [PS[m // 2][:, 512 * (m % 2):512 * (m % 2) + 512] for m in range(6)]
                    for n in range(4):
                        o = product_rows(n % 2, 2, 2 * n, 512, range(6), lambda m: vb[m], n == 0, n == 3,
                                         (rq, rk, kc, gr[1]) if n == 0 else ())
                        refill(n % 2, nx(8 + n))
                        if n == 0:
                            dc = decay()
                    wait(AC, o)
                    wait(VE, o)
                    for m in range(6):
                        if m % 2:
                            vd = inc(VE.tensor_copy(V[:, m, :], vb[m]), "dve")
                        else:
                            vr = inc(AC.activation(V[:, m, :], vb[m], ACT.Copy), "act")
                        if m == 1:
                            v01 = (vd, vr)
                    rd = [None] * 4
                    for m in range(6):
                        d = PS[(3, 0)[(m % 4) // 2]][:, 512 * (m % 2):512 * (m % 2) + 512]
                        wait(PE, rd[m % 4], *(v01 if m == 2 else ()))
                        for a in range(2):
                            mm = PE.matmul(d, K[:, a, m * P:(m + 1) * P], Q[:, a, :], start=(a == 0), stop=(a == 1))
                        sc = inc(mm, "pe")
                        if m < 4:
                            mt = DC[:, -U0 - P * m:-U0 - P * m + S]
                        else:
                            jj = m - 4
                            f0, b0 = L - P * jj - U0, -S - P * jj - U0
                            wait(VE, dc, rd[0])
                            mc = inc(VE.tensor_tensor(MC[:, :], DC[:, f0:f0 + S], DC[:, b0:b0 + S], ALU.add), "dve")
                            wait(VE, mc)
                            mt = MC[:, :]
                        wait(VE, sc)
                        rd[m % 4] = inc(VE.scalar_tensor_tensor(AT[:, m, :], d, 256 ** -0.5, mt, ALU.mult, ALU.mult), "dve")
                        if m >= 4:
                            wait(VE, rd[m % 4])
                    wait(PE, rd[1], vr, vd)
                    for e in range(4):
                        d = PS[2 - e // 2][:, 512 * (e % 2):512 * (e % 2) + 512]
                        for m in range(6):
                            mm = PE.matmul(d, V[:, m, e * P:(e + 1) * P], AT[:, m, :], start=(m == 0), stop=(m == 5))
                        ov = inc(mm, "pe")
                        wait(AC, ov)
                        oc = inc(AC.activation(O[:, e, :], d, ACT.Copy), "act")
                    wait(PE, oc, rd[1], on)
                    for e in range(4):
                        mm = PE.matmul(PS[0][:, 0:S], ON[:, :], O[:, e, :], start=(e == 0), stop=(e == 3))
                    mu = inc(mm, "pe")
                    wait(VE, mu)
                    g2 = product(0, PS[3][:, 0:512], (HH, HL), KT, IMG)
                    for e in range(4):
                        cen = inc(VE.tensor_tensor(O[:, e, :], O[:, e, :], PS[0][:, 0:S], ALU.subtract), "dve")
                        wait(AC, cen)
                        sq = inc(AC.activation(AT[:, e, :], O[:, e, :], ACT.Square), "act")
                        wait(PE, sq)
                        mm = PE.matmul(PS[0][:, S:2 * S], ON[:, :], AT[:, e, :], start=(e == 0), stop=(e == 3))
                    var = inc(mm, "pe")
                    g3 = product(1, PS[3][:, 512:1024], (HH, HL), KT, IMG)
                    gate_read(2, PS[3][:, 0:512], g2, nx(12))
                    ri = rsqrt(AT[:, 4, :], PS[0][:, S:2 * S], AT[:, 5, :], var)
                    gate_read(3, PS[3][:, 512:1024], g3, nx(13))
                    gated = [None] * 4
                    for e in range(4):
                        wait(PO, sq, gr[e])
                        gated[e] = inc(PO.tensor_tensor(O[:, e, :], O[:, e, :], G[:, e, :], ALU.mult), "pool")
                    wait(VE, ri)
                    ys, yh = [None] * 4, [None] * 4
                    for e in range(5):
                        if e < 4:
                            gain = GG[:, bass.ds(h * 4 + e, 1)]
                            wait(VE, gated[e])
                            y = inc(VE.scalar_tensor_tensor(O[:, e, :], O[:, e, :], gain, AT[:, 4, :], ALU.mult, ALU.mult), "dve")
                            wait(AC, y)
                            yh[e] = inc(AC.activation(YH[:, e, :], O[:, e, :], ACT.Copy), "act")
                        if e > 0:
                            wait(VE, yh[e - 1])
                            ys[e - 1] = inc(VE.tensor_tensor(YL[:, e - 1, :], O[:, e - 1, :], YH[:, e - 1, :].bitcast(F32),
                                                             ALU.subtract), "dve")
                    wait(PE, ri, *gr[2:])
                    orr = [None, None]
                    for n in range(4):
                        half = n % 2
                        wait(PE, c.now(f"lo{half}"), orr[half])
                        for u in range(2):
                            i = 0
                            for k in range(4):
                                wait(PE, ys[k])
                                for wt, y in ((WH, YH), (WH, YL), (WL, YH)):
                                    col = (u * 4 + k) * P
                                    mm = PE.matmul(PS[half][:, 512 * u:512 * u + 512], wt[half][:, col:col + P], y[:, k, :],
                                                   start=(i == 0), stop=(i == 11))
                                    i += 1
                        o = inc(mm, f"mm{half}")
                        refill(half, nx(14 + n))
                        wait(VE, o)
                        for u in range(2):
                            orr[half] = inc(VE.scalar_tensor_tensor(X[:, 2 * n + u, 0:S], PS[half][:, 512 * u:512 * u + 512],
                                                                    MOD[:, 1, 16 + 2 * n + u, 0:1], X[:, 2 * n + u, 0:S],
                                                                    ALU.mult, ALU.add), "dve")
                c.barrier()

        def trunk_mixers(l, ready):
            segs = ALL if l == 2 else IMG
            n, nt = segs[-1][1], segs[-1][1] // P
            win = dram[f"zin{l}"]
            lam0 = 0.8 - 0.6 * float(np.exp(-0.3 * (l - 2)))

            def unit(u):
                return win[u], UNIT

            def flat(t, a, b):
                return t[:, a:b, :].rearrange("p a b -> p (a b)")

            with ExitStack() as st:
                Z = sb(f"Z{l}", [P, 12, T], F32, st)
                DK = sb(f"DK{l}", [P, 2, T], F32, st)
                AV = sb(f"AV{l}", [P, 6, L], F32, st)
                DV = sb(f"DV{l}", [P, 6, L], F32, st)
                BD = sb(f"BD{l}", [P, P], F32, st)
                SG = sb(f"SLG{l}", [P, 1], F32, st)
                LQ = sb(f"LQ{l}", [P, 4, 32], F32, st)
                LAM = sb(f"LAM{l}", [P, 4], F32, st)
                ID = sb(f"dID{l}", [P, P], F32, st)
                c.barrier(AC, VE, PO)
                c.barrier(SP)
                inc(SP.dma_start(BD[:, :], dram["bd64"]), "small", by=16)
                inc(SP.dma_start(SG[:, :], dram["subln"][l - 2]), "small", by=16)
                tab = inc(SP.dma_start(LQ[:, :, :], dram["lambda"][l - 2]), "small", by=16)

                with ExitStack() as s2:
                    T1 = sb(f"mT1{l}", [P, T], F32, s2)
                    T2 = sb(f"mT2{l}", [P, T], F32, s2)
                    RT = sb(f"mRT{l}", [P, S], F32, s2)
                    WS = sb(f"WS{l}", [P, 4, P], F32, s2)
                    BS = sb(f"BS{l}", [P, 2, P], F32, s2)
                    COS = sb(f"mCOS{l}", [P, S], F32, s2)
                    SIN = sb(f"mSIN{l}", [P, S], F32, s2)
                    SW = sb(f"SW{l}", [P, 2, 3], F32, s2)
                    MS = [sb(f"MS{l}{i}", [P, 24], F32, s2) for i in range(3)]
                    CS = sb(f"CS{l}", [P, 2 * P], F32, s2)
                    CN = sb(f"CN{l}", [P, 2, 4, S], F32, s2)
                    Y = sb(f"Y{l}", [P, 4, 2, 2 * P], F32, s2)
                    inc(SP.dma_start(WS[:, :, :], dram["gmlp_w"][l - 2]), "small", by=16)
                    inc(SP.dma_start(BS[:, :, :], dram["gmlp_b"][l - 2]), "small", by=16)
                    inc(SP.dma_start(COS[:, :], dram["cos32"]), "small", by=16)
                    inc(SP.dma_start(SIN[:, :], dram["sin32"]), "small", by=16)
                    inc(SP.dma_start(CS[:, :], dram["dft64"]), "small", by=16)
                    inc(SP.dma_start(ID[:, :], dram["ident"]), "small", by=16)
                    tab = inc(SP.dma_start(SW[:, :, :], dram["sconv"][l - 2]), "small", by=16)

                    banks = [PS[m // 2][:, 512 * (m % 2):512 * (m % 2) + L] for m in range(6)]
                    for u in range(2):
                        o = product_rows(u, 4, 4 * u, L, range(nt), lambda m: banks[m], u == 0, u == 1, (), ready)
                        refill(u, unit(2 + u))
                    wait(AC, o)
                    for m in range(nt):
                        av = inc(AC.activation(AV[:, m, :], banks[m], ACT.Gelu_apprx_tanh), "act")
                    wait(PE, av)
                    wait(VE, tab)
                    v = inc(VE.tensor_tensor(LQ[:, 0:2, :], LQ[:, 0:2, :], LQ[:, 2:4, :], ALU.mult), "dve")
                    wait(VE, v)
                    v = inc(VE.reduce_sum(LAM[:, 0:2], LQ[:, 0:2, :], AX), "dve")
                    wait(AC, v)
                    e = inc(AC.activation(LAM[:, 0:2], LAM[:, 0:2], ACT.Exp), "act")
                    wait(VE, e)
                    v = inc(VE.tensor_tensor(LAM[:, 2:3], LAM[:, 0:1], LAM[:, 1:2], ALU.subtract), "dve")
                    wait(VE, v)
                    v = inc(VE.tensor_scalar(LAM[:, 2:3], LAM[:, 2:3], lam0, -1.0, ALU.add, ALU.mult), "dve")
                    inc(VE.tensor_scalar(SG[:, :], SG[:, :], 1.0 - lam0, None, ALU.mult), "dve")

                    def tile(i, half, free, dst, sg, nx):
                        o = product(half, PS[half], (HH, HL), KT, sg, (free,))
                        refill(half, nx)
                        wait(AC, o)
                        inc(AC.activation(dst, PS[half][:, 0:sg[-1][1]], ACT.Copy), "act", f"z_read{half}")

                    with c.fori(f"z{l}", 6) as i:
                        for half in range(2):
                            tile(i, half, c.prev(f"z_read{half}"), at(Z, i * 2 + half, 0, n), segs, unit(i * 2 + (half + 4)))

                    def gate_norm():
                        g = 4 * nt
                        ms, m1, m2 = (t[:, 0:g] for t in MS)
                        for q, t in enumerate((T1, T2)):
                            mm = nt // 2
                            sq = inc(AC.activation(t[:, 0:mm * L], flat(AV, q * mm, (q + 1) * mm), ACT.Square), "act")
                            wait(VE, sq)
                            v = inc(VE.reduce_sum(MS[0][:, q * 4 * mm:(q + 1) * 4 * mm],
                                                  t[:, 0:mm * L].rearrange("p (a b) -> p a b", b=64), AX), "dve")
                        wait(VE, v)
                        v = inc(VE.tensor_scalar(ms, ms, 1.0 / 64, None, ALU.mult), "dve")
                        r = rsqrt(m1, ms, m2, v)
                        wait(VE, r)
                        av4 = AV[:, 0:nt, :].rearrange("p m (h d) -> p (m h) d", d=64)
                        return inc(VE.tensor_tensor(av4, av4, m1.unsqueeze(2).to_broadcast([P, g, 64]), ALU.mult), "dve")

                    def rope_shuffle(t):
                        q = Z[:, 10 + t, 0:S] if t < 2 else DK[:, t - 2, 0:S]
                        wait(VE, c.last.get("roped"), zr)
                        VE.sem_inc(c.sem("held"), 1)
                        sw = inc(VE.stream_shuffle(RT[:, :], q, [i ^ 8 for i in range(32)]), "dve")
                        wait(PO, sw)
                        inc(PO.tensor_tensor(q, q, COS[:, :], ALU.mult), "pool")
                        r = inc(PO.tensor_tensor(RT[:, :], RT[:, :], SIN[:, :], ALU.mult), "pool")
                        wait(PO, r)
                        inc(PO.tensor_tensor(q, q, RT[:, :], ALU.add), "pool", "roped")

                    cn = inc(SP.dma_start(CN[:, :, :, :], dram["dft512"]), "dft", by=16)
                    zr = c.last["z_read1"]
                    tile(12, 0, c.last["z_read0"], DK[:, 0, :], ALL, unit(16))
                    for e in (PE, VE, PO, AC):
                        wait(e, tab)
                    c.last.pop("roped", None)
                    wait(VE, zr)
                    wait(AC, zr)
                    u_ = inc(AC.activation(Z[:, 0:2, 0:n], Z[:, 0:2, 0:n], ACT.Gelu_apprx_tanh), "act")
                    avn = gate_norm()
                    rope_shuffle(0)
                    tile(12, 1, c.last["z_read1"], DK[:, 1, :], ALL, unit(17))
                    zr = c.last["z_read1"]
                    wait(PE, avn)
                    mixed = [PS[3], PS[2]]
                    for t in (1, 0):
                        for h in (2 * t, 2 * t + 1):
                            for m in range(nt):
                                mm = PE.matmul(mixed[t][64 * (h % 2):64 * (h % 2) + 64, m * P:(m + 1) * P],
                                               AV[:, m, 64 * h:64 * h + 64], WS[:, h, :], start=True, stop=True)
                        mx = inc(mm, "pe")
                        tt = (T1, T2)[t]
                        wait(VE, mx, u_)
                        va = inc(VE.tensor_tensor(tt[:, 0:n].rearrange("p (m q) -> p m q", q=P),
                                                  mixed[t][:, 0:n].rearrange("p (m q) -> p m q", q=P),
                                                  BS[:, t:t + 1, :].to_broadcast([P, nt, P]), ALU.add), "dve", f"mix_read{t}")
                    for t in (1, 0):
                        tt = (T1, T2)[t]
                        wait(VE, c.last[f"mix_read{t}"])
                        gated = inc(VE.tensor_tensor(Z[:, t, 0:n], tt[:, 0:n], Z[:, t, 0:n], ALU.mult), "dve")
                    rope_shuffle(1)

                    wait(PE, c.last["z_read1"])
                    for u in range(2):
                        o = product_rows(u, 4, 4 * u, L, range(6), lambda m: banks[m], u == 0, u == 1,
                                         (c.last["mix_read1"], c.last["z_read0"], c.last["z_read1"]))
                        refill(u, (dram[f"zout{l}"][u], UNIT))
                        rope_shuffle(2 + u)

                        v = inc(VE.tensor_tensor(T1[:, 0:n], Z[:, 6 + u, 0:n], Z[:, 2 + u, 0:n], ALU.mult), "dve")
                        wait(AC, v, gated, c.last.get("conv_done"))
                        ct = inc(AC.activation(T2[:, 0:n], T1[:, 0:n], ACT.Copy, scale=SW[:, u, 1:2]), "act")
                        wait(VE, ct)
                        for a, b, _ in segs:
                            v = inc(VE.scalar_tensor_tensor(T2[:, a + 1:b], T1[:, a:b - 1], SW[:, u, 0:1],
                                                            T2[:, a + 1:b], ALU.mult, ALU.add), "dve")
                        wait(VE, v)
                        for a, b, _ in segs:
                            v = inc(VE.scalar_tensor_tensor(T2[:, a:b - 1], T1[:, a + 1:b], SW[:, u, 2:3],
                                                            T2[:, a:b - 1], ALU.mult, ALU.add), "dve")
                        wait(VE, v)
                        v = inc(VE.tensor_tensor(Z[:, 4 + u, 0:n], T2[:, 0:n], Z[:, 4 + u, 0:n], ALU.mult), "dve", "conv_done")
                        wait(VE, v)
                    wait(AC, o)
                    for m in range(6):
                        dv = inc(AC.activation(DV[:, m, :], banks[m], ACT.Copy), "act")

                    def features_dft(ms, free):
                        for i, m in enumerate(ms):
                            wait(PE, free[i % 2])
                            for t in range(2):
                                mm = PE.matmul(PS[i % 2][:, 512 * t:512 * t + 2 * P], Z[:, 8 + t, m * P:(m + 1) * P], CS[:, :],
                                               start=True, stop=True)
                            o = inc(mm, "pe")
                            wait(AC, o)
                            free[i % 2] = inc(AC.activation(Y[:, i, :, :], PS[i % 2][:, :].rearrange(
                                "p (t d) -> p t d", t=2)[:, :, 0:2 * P], ACT.Copy), "act")
                        wait(PE, free[0], free[1])

                    def tokens_dft(t, a, cn, nm, w):
                        i = 0
                        for m in range(nm):
                            for q in range(2):
                                mm = PE.matmul(PS[2 + t][:, a:a + w], Y[:, m, t, q * P:(q + 1) * P], cn(q, m),
                                               start=(i == 0), stop=(i == 2 * nm - 1))
                                i += 1
                        return inc(mm, "pe")

                    wait(AC, gated, c.last["conv_done"])
                    wait(VE, o)
                    features_dft(range(4), [dv, dv])
                    for t, zt in ((0, 0), (1, 1), (2, 4), (3, 5)):
                        split(HH[:, t, 0:n], HL[:, t, 0:n], Z[:, zt, 0:n], c.last["conv_done"])
                    wait(PE, cn)
                    for t in range(2):
                        o = tokens_dft(t, 0, lambda q, m: CN[:, q, m, :], 4, S)
                        split(HH[:, 4 + t, 0:S], HL[:, 4 + t, 0:S], PS[2 + t][:, 0:S], o)
                    if n > S:
                        wait(SP, o)
                        wait(AC, o)
                        cc = CN[:, :, 0, :].rearrange("p q (m k) -> p q m k", m=2)
                        tab = inc(SP.dma_start(CN[:, :, 0, :], dram["dft256"]), "dft", by=16)
                        features_dft((4, 5), [None, None])
                        wait(PE, tab, c.now("dve"))
                        for t in range(2):
                            o = tokens_dft(t, S, lambda q, m: cc[:, q, m, :], 2, L)
                            split(HH[:, 4 + t, S:T], HL[:, 4 + t, S:T], PS[2 + t][:, S:T], o)
                    c.barrier()

                with ExitStack() as s2:
                    QS = sb(f"dQS{l}", [P, 2, 2 * P], F32, s2)
                    PR = [[sb(f"dP{l}{m}{i}", [P, T], F32, s2) for i in range(3 - m)] for m in range(2)]
                    PT = [sb(f"dPT{l}{i}", [P, 6, P], F32, s2) for i in range(2)]
                    OD = sb(f"dOD{l}", [P, 2, T], F32, s2)
                    NM = sb(f"dNM{l}", [P, 8, 2], F32, s2)
                    RL = sb(f"dRL{l}", [P, 8, 2], F32, s2)
                    def blocks(qs, k0, m0, nm, dst):
                        w = nm * P
                        tok = {}

                        def scores(n):
                            q, h = n // 4, n % 4
                            for mp in range(2):
                                wait(PE, tok.get(("exp", n - 1, mp)))
                                r = slice(64 * (h % 2) + 32 * mp, 64 * (h % 2) + 32 * mp + 32)
                                for a in range(0, w, 512):
                                    b = min(w, a + 512)
                                    mm = PE.matmul(PS[mp][:, a:b], qs[r, h // 2, q * P:(q + 1) * P], DK[r, h // 2, k0 + a:k0 + b],
                                                   start=True, stop=True, tile_position=(r.start, 0))
                                tok["s", n, mp] = inc(mm, "pe")

                        def softmax(n):
                            for mp in range(2):
                                nmx = NM[:, n, mp:mp + 1]
                                wait(VE, tok["s", n, mp])
                                v = inc(VE.reduce_max(nmx, PS[mp][:, 0:w], AX), "dve")
                                wait(VE, v)
                                v = inc(VE.tensor_scalar(nmx, nmx, -(32 ** -0.5), None, ALU.mult), "dve")
                                wait(AC, v, tok.get(("t", n - 3)) if mp == 0 else tok.get(("p", n - 2)))
                                tok["exp", n, mp] = inc(AC.activation(PR[mp][n % (3 - mp)][:, 0:w], PS[mp][:, 0:w], ACT.Exp, bias=nmx,
                                                                      scale=32 ** -0.5, accum_out=RL[:, n, mp:mp + 1]), "act")

                        def combine(n):
                            p0, p1, r = PR[0][n % 3], PR[1][n % 2], RL[:, n, :]
                            wait(VE, tok["exp", n, 1])
                            v = inc(VE.reciprocal(r, r), "dve")
                            wait(VE, v)
                            v = inc(VE.tensor_tensor(r[:, 1:2], r[:, 1:2], LAM[:, 2:3], ALU.mult), "dve")
                            v0 = inc(VE.tensor_scalar(p0[:, 0:w], p0[:, 0:w], r[:, 0:1], None, ALU.mult), "dve")
                            wait(VE, v0)
                            tok["p", n] = inc(VE.scalar_tensor_tensor(p0[:, 0:w], p1[:, 0:w], r[:, 1:2], p0[:, 0:w],
                                                                      ALU.mult, ALU.add), "dve")

                        def turn(n):
                            wait(PE, tok["p", n], tok.get(("e", n - 1)))
                            for m in range(nm):
                                mm = PE.transpose(PS[2][:, m * P:(m + 1) * P], PR[0][n % 3][:, m * P:(m + 1) * P], ID[:, :])
                            tok["t", n] = inc(mm, "pe")
                            wait(AC, tok["t", n], tok.get(("av", n - 2)))
                            tok["e", n] = inc(AC.activation(PT[n % 2][:, 0:nm, :], PS[2][:, 0:w].rearrange(
                                "p (a b) -> p a b", b=P), ACT.Copy), "act")

                        def values(n):
                            q, h = n // 4, n % 4
                            wait(PE, tok["e", n])
                            for m in range(nm):
                                mm = PE.matmul(PS[3][64 * (h % 2):64 * (h % 2) + 64, 512 * q + (h // 2) * P:512 * q + (h // 2 + 1) * P],
                                               DV[:, m0 + m, 64 * h:64 * h + 64], PT[n % 2][:, m, :], start=(m == 0), stop=(m == nm - 1))
                            tok["av", n] = inc(mm, "pe")
                            if h == 3:
                                wait(AC, tok["av", n])
                                inc(AC.activation(dst(q), PS[3][:, 512 * q:512 * q + 2 * P].rearrange("p (t q) -> p t q", t=2),
                                                  ACT.Copy), "act")

                        for step in range(8 + 3):
                            if step < 8:
                                scores(step)
                                softmax(step)
                            if 0 <= step - 1 < 8:
                                combine(step - 1)
                            if 0 <= step - 2 < 8:
                                turn(step - 2)
                            if 0 <= step - 3 < 8:
                                values(step - 3)

                    with c.fori(f"diff{l}", S // P // 2) as b:
                        c.barrier()
                        v = inc(VE.tensor_copy(QS[:, :, :], Z[:, 10:12, bass.ds(b * 2 * P, 2 * P)]), "dve")
                        wait(PE, v)
                        blocks(QS, 0, 0, 6, lambda q: OD[:, :, bass.ds(b * 2 * P + q * P, P)])
                    c.barrier()
                    if n > S:
                        blocks(Z[:, 10:12, S:T], S, 4, 2, lambda q: OD[:, :, S + q * P:S + (q + 1) * P])
                    c.barrier()
                    N = [*PR[0], PR[1][0]]
                    done = [None] * 6
                    for t in range(2):
                        sq = inc(AC.activation(N[t][:, 0:n], OD[:, t, 0:n], ACT.Square), "act")
                        wait(PE, sq)
                        for a, b, _ in segs:
                            mm = PE.matmul(PS[2 + t][:, a:b], BD[:, :], N[t][:, a:b], start=True, stop=True)
                        sq = inc(mm, "pe", f"d_var{t}")
                    for t in range(2):
                        r = rsqrt(N[2 + t][:, 0:n], PS[2 + t][:, 0:n], N[t][:, 0:n], c.last[f"d_var{t}"], dve="norm_dve")
                        wait(VE, r)
                        v = inc(VE.scalar_tensor_tensor(OD[:, t, 0:n], OD[:, t, 0:n], SG[:, 0:1], N[2 + t][:, 0:n],
                                                        ALU.mult, ALU.mult), "norm_dve")
                        done.append(split(HH[:, 6 + t, 0:n], HL[:, 6 + t, 0:n], OD[:, t, 0:n], v, dve="norm_dve"))
            return done

        def final_norm(wk):
            with ExitStack() as st:
                RS = sb("fRS", [P, S], F32, st)
                RI = sb("fRI", [P, S], F32, st)
                FG = sb("fFG", [P, KT], F32, st)
                c.barrier(SP, VE, AC)
                tab = inc(SP.dma_start(FG[:, :], dram["finalg"]), "small", by=16)
                r = rsqrt(RI[:, :], PS[2][:, 0:S], RS[:, :], mean_square(S, IMG, wk, True))
                wait(VE, r, tab)
                for k in range(KT):
                    v = inc(VE.scalar_tensor_tensor(X[:, k, 0:S], X[:, k, 0:S], FG[:, k:k + 1], RI[:, :], ALU.mult, ALU.mult), "dve")
                    wait(SP, v)
                    inc(SP.dma_start(out[k], X[:, k, 0:S]), "stored", by=16)
                wait(SP, c.now("stored"))

        def first(name, n=1):
            return tuple((dram[name][i * n], UNIT) for i in range(2))

        def first_refills(name):
            for slot, unit in enumerate(first(name)):
                refill(slot, unit)

        @contextmanager
        def work():
            with ExitStack() as st:
                yield [sb(f"WK{c.cnt['pe']}_{i}", [P, T], F32, st) for i in range(3)]

        A0 = 4
        with ExitStack() as st:
            buf = [sb(f"AR0{i}", [P, 4, 512], F32, st) for i in range(2)] + [sb("EV0", [P, 512], F32, st)]
            buf = (buf[0][:, :, :], buf[1][:, :, :], buf[2][:, :])
            ada_start(0, buf)
            inc(SP.dma_start(X[:, :, :], dram["xt"].rearrange("p (k t) -> p k t", k=KT)), "xin", by=16)
            with c.fori("ada0", A0 - 1) as i:
                ada_sum(0, i, buf)
                ada_next(0, i, buf)
                ada_turn(i, buf)
            ada_sum(0, A0 - 1, buf)
            ada_turn(A0 - 1, buf)
            ada_finish(0, 0, 4 * A0)
        first_refills("wqkv")
        with work() as wk:
            c.barrier(SP)
            ready = norm("0a", 0, 0, ALL, wk, False)
        attention(ready)
        with work() as wk:
            project("0", 0, 16, lambda n: dram["wo0"][n], ALL, first("win0"), wk)
            c.barrier(SP)
            ready = norm("0b", 0, 1, ALL, wk, True)
            ffn("0", 0, ALL, first("wret"), wk, ready, ada=1)
            ready = norm("1a", 1, 0, ALL, wk, True)
        retention(ready)
        with work() as wk:
            c.barrier(SP)
            ready = norm("1b", 1, 1, IMG, wk, False)
            ffn("1", 1, IMG, first("zin2"), wk, ready, ada=2)
        c.barrier(SP)
        wait(SP, c.now("xin"))
        c2 = inc(SP.dma_start(X[:, :, S:T], dram["xc2"].rearrange("p (k t) -> p k t", k=KT)), "xin", by=16)
        for e in (VE, AC, PO):
            wait(e, c2)
        for l in (2, 3):
            segs = ALL if l == 2 else IMG
            if l == 2:
                with work() as wk:
                    ready = norm("2a", 2, 0, ALL, wk, False)
            ready = trunk_mixers(l, ready)
            with work() as wk:
                project(f"{l}", l, 16, lambda u: dram[f"zout{l}"][u], segs, first(f"win{l}"), wk, ready)
                c.barrier(SP)
                ready = norm(f"{l}b", l, 1, segs, wk, True)
                ffn(f"{l}", l, segs, first("zin3") if l == 2 else (None, None), wk, ready, CW[:, l - 2, :, :],
                    ada=3 if l == 2 else None)
                if l == 2:
                    ready = norm("3a", 3, 0, ALL, wk, True)
                else:
                    final_norm(wk)


def rotary(dim, feature):
    f = np.float32
    half = dim // 4
    n = np.arange(S)
    inv = (f(10000.0) ** (-np.arange(0, dim // 2, 2, dtype=f) / f(dim // 2))).astype(f)
    pos = np.where(feature[:, None] < dim // 2, (n // 64)[None], (n % 64)[None]).astype(f)
    ang = pos * inv[feature % half][:, None]
    sign = np.where(feature % (dim // 2) < half, -1.0, 1.0).astype(f)[:, None]
    return np.cos(ang).astype(f), (np.sin(ang) * sign).astype(f)


def layout(x):
    f = np.float32
    a = {k: np.asarray(v) for k, v in x.items()}

    def cols(v):
        v = v.reshape(*v.shape[:-1], -1, P)
        return np.swapaxes(v, -1, -2)

    d = {}
    xt = np.concatenate([a["x"][0], a["ctx"][0]], 0).T
    d["xt"] = xt.reshape(KT, P, T).transpose(1, 0, 2).reshape(P, KT * T)
    cin = np.stack([np.stack([a["c"][0], a["c_ctx"]], 0), np.stack([a["c_2"][0], a["c_ctx_2"]], 0)], 0)
    d["cin"] = cin.reshape(2, 2, KT, P).transpose(3, 0, 2, 1).reshape(P, -1)
    adb = np.concatenate([a["ada_b"], a["b_ada_2"]], 0)
    d["adb"] = adb.reshape(4, NV, P).transpose(2, 0, 1).reshape(P, -1)
    g = np.stack([np.concatenate([a["norm1_g"], a["norm1_g_2"]], 0), np.concatenate([a["norm2_g"], a["norm2_g_2"]], 0)], 1)
    d["gn"] = g.reshape(4, 2, KT, P).transpose(3, 0, 1, 2).reshape(P, -1)
    sel = np.zeros((P, 2), f)
    for q in range(4):
        for j in range(2):
            sel[32 * q + j, j] = 1
    d["sel"] = sel
    w = np.concatenate([a["ada_w"], a["w_ada_2"]], 0)
    d["ada"] = w.reshape(4, 2, 4, P, 12, 512).transpose(0, 4, 1, 3, 2, 5).reshape(96, P, 4, 512)

    def units(w, kt):
        n = w.shape[1] // P
        return w.reshape(kt, P, n, P).transpose(2, 1, 0, 3).reshape(n, P, kt * P)

    w = a["attn_w_qkv"][0]
    heads = [h for p in range(2) for j in range(4) for h in ((2 * p) * 4 + j, (2 * p + 1) * 4 + j)]
    order = np.concatenate([np.arange(h * 64, h * 64 + 64) for h in heads])
    wv = w[:, 1280:].reshape(2, 4, P, L).transpose(0, 2, 1, 3).reshape(2, P, UNIT)
    d["wqkv"] = np.concatenate([units(w[:, order], KT), units(w[:, 1024:1280], KT), wv], 0)
    d["wo0"] = units(a["attn_w_o"][0][order], KT)
    d["sink"] = a["attn_sink"][0][heads].reshape(1, 16)
    d["qkgain"] = np.stack([np.tile(a["attn_q_norm"][0], 2), np.tile(a["attn_k_norm"][0], 2)], 1)
    d["bd64"] = np.kron(np.eye(2, dtype=f), np.full((64, 64), 1 / 64, f))
    d["ident"] = np.eye(P, dtype=f)
    d["cos64"], d["sin64"] = rotary(64, np.arange(P) % 64)
    r, n = np.arange(P)[:, None], np.arange(3 * P)[None, :]
    mask = []
    for b in range(4):
        key = b * P - P + n
        mask.append(np.where((n >= r) & (n - r <= 2 * P) & (key >= 0) & (key < S), 0.0, -1e31))
    d["mask"] = np.stack(mask, 1).reshape(P, -1).astype(f)
    w, wo = a["ret_w_qkvg"][0], a["ret_w_o"][0]
    pair = np.concatenate([np.arange(64), np.arange(128, 192), np.arange(64, 128), np.arange(192, 256)])
    parts = []
    for h in range(4):
        parts.append(units(w[:, 256 * h + pair], KT))
        parts.append(units(w[:, D + 256 * h + pair], KT))
        parts.append(units(w[:, 4 * D + 512 * h:4 * D + 512 * h + 256], KT))
        parts.append(w[:, 2 * D + 512 * h:2 * D + 512 * (h + 1)].reshape(4, 2, P, 512).transpose(0, 2, 1, 3).reshape(4, P, UNIT))
        parts.append(units(w[:, 4 * D + 512 * h + 256:4 * D + 512 * (h + 1)], KT))
        u = wo[512 * h:512 * (h + 1)].reshape(4, P, 4, 2, P).transpose(2, 1, 3, 0, 4)
        parts.append(u.reshape(4, P, UNIT))
    wi = units(a["ffn_w_in"][1], KT)
    d["wret"] = np.concatenate(parts + [wi[0:1], wi[FT:FT + 1]], 0)
    fi = np.arange(P)
    d["cos256"], s256 = rotary(256, np.where(fi < 64, fi, fi + 64))
    d["sin256"] = -s256
    d["gngain"] = a["ret_gn_g"][0].reshape(16, P).T
    d["decay"] = np.broadcast_to(a["ret_decay_logit"][0].reshape(8), (P, 8))
    d["dist"] = (np.arange(-(S + P), L + S)[None, :] - np.arange(P)[:, None]).astype(f)
    d["xc2"] = a["ctx_2"][0].T.reshape(KT, P, L).transpose(1, 0, 2).reshape(P, KT * L)
    rows = lambda w: w.reshape(2, 4, P, L).transpose(0, 2, 1, 3).reshape(2, P, UNIT)
    for l in (2, 3):
        w = a["w_in_2"][l - 2]
        g = lambda i: w[:, i * 256:(i + 1) * 256]
        feats = np.concatenate([g(i) for i in (0, 2, 3, 4, 5, 6, 7)], 1)
        d[f"zin{l}"] = np.concatenate([rows(g(1)), units(feats, KT), rows(g(8))], 0)
        d[f"zout{l}"] = units(a["w_out_2"][l - 2], KT)
    d["gmlp_w"] = a["gmlp_ws_2"].transpose(0, 3, 1, 2)
    d["gmlp_b"] = np.repeat(a["gmlp_bs_2"].reshape(2, 2, 2, P).transpose(0, 2, 1, 3), 64, axis=1)
    d["sconv"] = a["sconv_w_2"].reshape(2, 3, 2, P).transpose(0, 3, 2, 1)
    d["ffnconv"] = a["ffn_conv_w_2"].reshape(2, 3, FT, P).transpose(3, 0, 2, 1)
    lam = np.stack([a["lambda_q1_2"], a["lambda_q2_2"], a["lambda_k1_2"], a["lambda_k2_2"]], 1)
    d["lambda"] = np.broadcast_to(lam[:, None], (2, P, 4, 32))
    d["subln"] = np.tile(a["subln_g_2"], (1, 2)).reshape(2, P, 1)
    d["finalg"] = a["final_g_2"].reshape(KT, P).T
    d["cos32"], d["sin32"] = rotary(32, np.arange(P) % 32)

    def dft(n, fn):
        i = np.arange(n)
        return fn(2 * np.pi * (np.outer(i, i) % n) / n) / np.sqrt(n)

    d["dft64"] = np.concatenate([np.kron(np.eye(2), dft(64, np.cos)), np.kron(np.eye(2), dft(64, np.sin))], 1).astype(f)
    for n in (S, L):
        cs = np.stack([dft(n, np.cos), -dft(n, np.sin)], 0)
        cs = cs.reshape(2, n // P, P, n).transpose(2, 0, 1, 3)
        d[f"dft{n}"] = (cs if n == S else cs.reshape(P, 2, 2 * L)).astype(f)
    for l in range(4):
        wi = (a["ffn_w_in"] if l < 2 else a["ffn_w_up_2"])[l % 2]
        u = units(wi, KT)
        d[f"win{l}"] = np.stack([u[:FT], u[FT:]], 1).reshape(2 * FT, P, UNIT)
        wd = (a["ffn_w_out"] if l < 2 else a["ffn_w_down_2"])[l % 2]
        d[f"wdn{l}"] = np.concatenate([units(wd[c * FC * P:(c + 1) * FC * P], FC) for c in range(CH)], 0)
    return {k: np.ascontiguousarray(v, dtype=v.dtype) for k, v in d.items()}


def program(shapes, nc_of):
    book = {}
    for dry in (True, False):
        nc = nc_of()
        dram = {k: nc.dram_tensor(f"in_{k}", s, F32, kind="ExternalInput").ap() for k, s in shapes.items()}
        out = nc.dram_tensor("out_x", (KT, P, S), F32, kind="ExternalOutput").ap()
        build(nc, dram, out, book, dry)
    return nc


def kernel(**inputs):
    import concourse.bacc as _bacc
    from concourse.bass_utils import run_bass_kernel_spmd as _run

    arrays = layout(inputs)
    nc = program({k: v.shape for k, v in arrays.items()},
                 lambda: _bacc.Bacc("TRN2", target_bir_lowering=False, num_devices=1))
    r = _run(nc, [{f"in_{k}": v for k, v in arrays.items()}], core_ids=[0])
    got = r.results[0]["out_x"]
    return np.ascontiguousarray(got.reshape(D, S).T.reshape(1, S, D))
```
